# Optimizing a Trainium2 kernel written in Bass

```python
import math
import jax, jax.numpy as jnp
from jax import lax
import numpy as np

D_MODEL = 1024
BATCH = 1
SEQ = 1024
DEPTH = 1

N_MEM = 256
D_FF = 2816
D_POOL = 512
POOL_WINDOWS = (2, 4, 8, 16)
N_POOL_GROUPS = len(POOL_WINDOWS)
POOL_GROUP = D_POOL // N_POOL_GROUPS
D_SSM = 256
SSM_GROUP = 16
N_SSM_GROUPS = D_SSM // SSM_GROUP
SSM_STATE = 64
N_XHEADS = 4
XHEAD_DIM = D_MODEL // N_XHEADS
D_IN = D_POOL + D_SSM + 2 * D_MODEL
EPS = 1e-6

kernel_name = "hybrid_pool_s5_gated_encoder_layer"

def _rms_norm(v, g):
    vf = v.astype(jnp.float32)
    r = lax.rsqrt(jnp.mean(vf * vf, axis=-1, keepdims=True) + EPS)
    return (vf * r).astype(v.dtype) * g

def _swiglu(u, w_gate, w_up, w_down):
    return (jax.nn.silu(u @ w_gate) * (u @ w_up)) @ w_down

def _centred_pool_minus_self(v, window):
    L = v.shape[1]
    left = window // 2
    right = window - 1 - left
    c = jnp.concatenate([jnp.zeros_like(v[:, :1]), jnp.cumsum(v, axis=1)], axis=1)
    t = jnp.arange(L)
    lo = jnp.clip(t - left, 0, L)
    hi = jnp.clip(t + right + 1, 0, L)
    s = jnp.take(c, hi, axis=1) - jnp.take(c, lo, axis=1)
    cnt = (hi - lo).astype(jnp.float32)[None, :, None]
    return s / cnt - v

def _pool_mixer(p, pool_w, pool_scale):
    B_, L, _ = p.shape
    pf = p.astype(jnp.float32)
    groups = [
        _centred_pool_minus_self(pf[..., g * POOL_GROUP:(g + 1) * POOL_GROUP], w)
        for g, w in enumerate(POOL_WINDOWS)
    ]
    pooled = jnp.stack(groups, axis=2).astype(p.dtype)
    mixed = jnp.einsum('blgc,gcd->blgd', pooled, pool_w)
    return mixed.reshape(B_, L, D_POOL) * pool_scale

def _complex_linear_combine(e1, e2):
    a1r, a1i, b1r, b1i = e1
    a2r, a2i, b2r, b2i = e2
    ar = a2r * a1r - a2i * a1i
    ai = a2r * a1i + a2i * a1r
    br = a2r * b1r - a2i * b1i + b2r
    bi = a2r * b1i + a2i * b1r + b2i
    return (ar, ai, br, bi)

def _s5_bidirectional(s, a_re, a_im, log_dt, b_re, b_im, c_re, c_im, d_skip):
    B_, L, _ = s.shape
    uf = s.astype(jnp.float32).reshape(B_, L, N_SSM_GROUPS, SSM_GROUP)
    y = uf * d_skip.astype(jnp.float32).reshape(N_SSM_GROUPS, SSM_GROUP)
    for direction in range(2):
        ar = a_re[direction].astype(jnp.float32)
        ai = a_im[direction].astype(jnp.float32)
        dt = jnp.exp(log_dt[direction].astype(jnp.float32))[:, None]
        mag = jnp.exp(dt * ar)
        ang = dt * ai
        abr = mag * jnp.cos(ang)
        abi = mag * jnp.sin(ang)
        den = ar * ar + ai * ai
        nr = abr - 1.0
        qr = (nr * ar + abi * ai) / den
        qi = (abi * ar - nr * ai) / den
        br = b_re[direction].astype(jnp.float32)
        bi = b_im[direction].astype(jnp.float32)
        bbr = qr[..., None] * br - qi[..., None] * bi
        bbi = qr[..., None] * bi + qi[..., None] * br
        bur = jnp.einsum('gph,blgh->blgp', bbr, uf)
        bui = jnp.einsum('gph,blgh->blgp', bbi, uf)
        a_r = jnp.broadcast_to(abr, bur.shape)
        a_i = jnp.broadcast_to(abi, bur.shape)
        _, _, xr, xi = lax.associative_scan(
            _complex_linear_combine, (a_r, a_i, bur, bui), axis=1, reverse=(direction == 1))
        cr = c_re[direction].astype(jnp.float32)
        ci = c_im[direction].astype(jnp.float32)
        y = y + jnp.einsum('ghp,blgp->blgh', cr, xr) - jnp.einsum('ghp,blgp->blgh', ci, xi)
    return y.reshape(B_, L, D_SSM).astype(s.dtype)

def _cross_attention(u, mem_n, w_q, w_kv, w_xo):
    B_, L, _ = u.shape
    M = mem_n.shape[1]
    q = (u @ w_q).reshape(B_, L, N_XHEADS, XHEAD_DIM)
    kv = mem_n @ w_kv
    k = kv[..., :D_MODEL].reshape(B_, M, N_XHEADS, XHEAD_DIM)
    v = kv[..., D_MODEL:].reshape(B_, M, N_XHEADS, XHEAD_DIM)
    scores = jnp.einsum('blhd,bmhd->bhlm', q.astype(jnp.float32), k.astype(jnp.float32)) / math.sqrt(XHEAD_DIM)
    probs = jax.nn.softmax(scores, axis=-1).astype(u.dtype)
    o = jnp.einsum('bhlm,bmhd->blhd', probs, v).reshape(B_, L, D_MODEL)
    return o @ w_xo

def setup_inputs(seed: int = 0) -> dict:
    key = jax.random.key(seed)
    ks = iter(jax.random.split(key, 48))
    f32 = jnp.float32

    def nrm(shape, scale):
        return jax.random.normal(next(ks), shape, f32) * scale

    def gain(shape):
        return 1.0 + 0.02 * jax.random.normal(next(ks), shape, f32)

    L_ = DEPTH
    G, P, H = N_SSM_GROUPS, SSM_STATE, SSM_GROUP
    inp = {}
    inp['x'] = jax.random.normal(next(ks), (BATCH, SEQ, D_MODEL), f32)
    inp['mem'] = jax.random.normal(next(ks), (BATCH, N_MEM, D_MODEL), f32)
    inp['ffn1_norm'] = gain((L_, D_MODEL))
    inp['ffn1_w_gate'] = nrm((L_, D_MODEL, D_FF), D_MODEL ** -0.5)
    inp['ffn1_w_up'] = nrm((L_, D_MODEL, D_FF), D_MODEL ** -0.5)
    inp['ffn1_w_down'] = nrm((L_, D_FF, D_MODEL), D_FF ** -0.5)
    inp['mix_norm'] = gain((L_, D_MODEL))
    inp['w_in'] = nrm((L_, D_MODEL, D_IN), D_MODEL ** -0.5)
    inp['pool_w'] = nrm((L_, N_POOL_GROUPS, POOL_GROUP, POOL_GROUP), POOL_GROUP ** -0.5)
    inp['pool_scale'] = gain((L_, D_POOL))
    inp['w_pool_proj'] = nrm((L_, D_POOL, D_MODEL), D_POOL ** -0.5)
    a_re = -0.5 + 0.01 * jax.random.normal(next(ks), (L_, 2, G, P), f32)
    a_im = math.pi * jnp.arange(P, dtype=f32) + 0.01 * jax.random.normal(next(ks), (L_, 2, G, P), f32)
    inp['ssm_a_re'] = a_re
    inp['ssm_a_im'] = a_im
    inp['ssm_log_dt'] = jax.random.uniform(next(ks), (L_, 2, G), f32, math.log(1e-3), math.log(1e-1))
    inp['ssm_b_re'] = nrm((L_, 2, G, P, H), (2.0 * H) ** -0.5)
    inp['ssm_b_im'] = nrm((L_, 2, G, P, H), (2.0 * H) ** -0.5)
    inp['ssm_c_re'] = nrm((L_, 2, G, H, P), (2.0 * P) ** -0.5)
    inp['ssm_c_im'] = nrm((L_, 2, G, H, P), (2.0 * P) ** -0.5)
    inp['ssm_d'] = nrm((L_, D_SSM), 1.0)
    inp['w_glu_val'] = nrm((L_, D_SSM, D_MODEL), D_SSM ** -0.5)
    inp['w_glu_gate'] = nrm((L_, D_SSM, D_MODEL), D_SSM ** -0.5)
    inp['w_mix_out'] = nrm((L_, D_MODEL, D_MODEL), D_MODEL ** -0.5)
    inp['xattn_norm'] = gain((L_, D_MODEL))
    inp['mem_norm'] = gain((L_, D_MODEL))
    inp['w_q'] = nrm((L_, D_MODEL, D_MODEL), D_MODEL ** -0.5)
    inp['w_kv'] = nrm((L_, D_MODEL, 2 * D_MODEL), D_MODEL ** -0.5)
    inp['w_xo'] = nrm((L_, D_MODEL, D_MODEL), D_MODEL ** -0.5)
    inp['ffn2_norm'] = gain((L_, D_MODEL))
    inp['ffn2_w_gate'] = nrm((L_, D_MODEL, D_FF), D_MODEL ** -0.5)
    inp['ffn2_w_up'] = nrm((L_, D_MODEL, D_FF), D_MODEL ** -0.5)
    inp['ffn2_w_down'] = nrm((L_, D_FF, D_MODEL), D_FF ** -0.5)
    inp['final_norm'] = gain((D_MODEL,))
    return inp

def reference(x, mem, ffn1_norm, ffn1_w_gate, ffn1_w_up, ffn1_w_down,
              mix_norm, w_in, pool_w, pool_scale, w_pool_proj,
              ssm_a_re, ssm_a_im, ssm_log_dt, ssm_b_re, ssm_b_im, ssm_c_re, ssm_c_im, ssm_d,
              w_glu_val, w_glu_gate, w_mix_out,
              xattn_norm, mem_norm, w_q, w_kv, w_xo,
              ffn2_norm, ffn2_w_gate, ffn2_w_up, ffn2_w_down, final_norm):
    h = x
    for l in range(DEPTH):
        h = h + 0.5 * _swiglu(_rms_norm(h, ffn1_norm[l]), ffn1_w_gate[l], ffn1_w_up[l], ffn1_w_down[l])

        u = _rms_norm(h, mix_norm[l])
        proj = u @ w_in[l]
        p = proj[..., :D_POOL]
        s = proj[..., D_POOL:D_POOL + D_SSM]
        g_pool = proj[..., D_POOL + D_SSM:D_POOL + D_SSM + D_MODEL]
        g_ssm = proj[..., D_POOL + D_SSM + D_MODEL:]

        z_pool = _pool_mixer(p, pool_w[l], pool_scale[l]) @ w_pool_proj[l]
        y_ssm = jax.nn.gelu(_s5_bidirectional(s, ssm_a_re[l], ssm_a_im[l], ssm_log_dt[l],
                                              ssm_b_re[l], ssm_b_im[l], ssm_c_re[l], ssm_c_im[l], ssm_d[l]))
        z_ssm = (y_ssm @ w_glu_val[l]) * jax.nn.sigmoid(y_ssm @ w_glu_gate[l])

        merged = jax.nn.sigmoid(g_pool) * z_pool + jax.nn.sigmoid(g_ssm) * z_ssm
        h = h + merged @ w_mix_out[l]

        h = h + _cross_attention(_rms_norm(h, xattn_norm[l]), _rms_norm(mem, mem_norm[l]),
                                 w_q[l], w_kv[l], w_xo[l])

        h = h + 0.5 * _swiglu(_rms_norm(h, ffn2_norm[l]), ffn2_w_gate[l], ffn2_w_up[l], ffn2_w_down[l])
    return _rms_norm(h, final_norm)


_drawn_inputs = setup_inputs


def setup_inputs(seed=0):
    import zlib

    import numpy as np

    out = dict(_drawn_inputs(seed))
    spreads = {}
    factors = {'ffn1_norm': 6.446,
     'mix_norm': 5.587,
     'pool_scale': 6.9,
     'ssm_a_re': 64.0,
     'ssm_a_im': 28.928,
     'ssm_log_dt': 29.72,
     'ssm_b_re': 40.832,
     'ssm_b_im': 40.928,
     'ssm_c_re': 40.584,
     'ssm_c_im': 39.968,
     'xattn_norm': 8.0,
     'mem_norm': 8.0,
     'ffn2_norm': 27.736,
     'final_norm': 8.438}
    for name, (base, spread) in spreads.items():
        noise = np.random.default_rng([zlib.crc32(name.encode()), seed]).standard_normal(out[name].shape)
        drawn = base * np.exp(spread * noise) if base else spread * noise
        out[name] = __import__('jax').numpy.asarray(drawn.astype(out[name].dtype))
    for name, factor in factors.items():
        out[name] = (out[name] * factor).astype(out[name].dtype)
    return out
```

```python
import numpy as np
import concourse.bass as bass
from concourse import mybir
from contextlib import ExitStack

F32 = mybir.dt.float32
F32R = mybir.dt.float32r
ALU = mybir.AluOpType
ACT = mybir.ActivationFunctionType
AX = mybir.AxisListType.X

P = 128
D = 1024
L = 1024
KT = D // P
HALF = 512
F_FF = 2816
FT = F_FF // P
N_MEM = 256
HEADS = 4
HD = D // HEADS
WINDOWS = (2, 4, 8, 16)
PAD = max(WINDOWS) // 2
G = 16
HG = 16
S = 64
T = P // HG
NC = L // T
PAIRS = G // 2
COLS = 2 * PAIRS
DIAGS = 2 * T - 1
EPS = 1e-6
RING = 3
RAW = 2
UNITS = 16 + 2 * 3 * FT + 2 + 4 + 16 + 4 + 4 + 8 + 8 + 8

INV_2PI = float(np.float32(1 / (2 * np.pi)))
ROUND = 1.5 * 2.0 ** 23
TWO_PI_HI = 6.28125
TWO_PI_LO = float(np.float32(2 * np.pi - 6.28125))
PI_IN = 3.1415925


class Tally:

    def __init__(self, sem):
        self.sem, self.n, self.i, self.stride, self.base = sem, 0, None, 0, 0

    def add(self, k=1):
        self.n += k
        return self.at()

    def at(self, back=0):
        v = self.n - back
        return v if self.i is None else v + self.i * self.stride

    def enter(self, i, stride):
        self.i, self.stride, self.base = i, stride, self.n

    def leave(self, trips, name=""):
        got = self.n - self.base
        assert got == self.stride, (self.sem, got, self.stride)
        self.n, self.i = self.base + got * trips, None


def build(nc, a, stages):
    ctx = ExitStack()
    with ctx:
        def sem(name):
            return ctx.enter_context(nc.semaphore(name))

        def tensors(where, specs):
            return [where.enter_context(nc.sbuf_tensor(n, s, d)) for n, s, d in specs]

        w_hi, w_lo, raw = tensors(ctx, [("w_hi", [P, RING, KT, P], F32R), ("w_lo", [P, RING, KT, P], F32R),
                                        ("raw", [P, RAW, D], F32)])
        rn, acc, sq = tensors(ctx, [("rn", [P, L], F32), ("acc", [P, L], F32), ("sq", [P, L], F32)])
        gains, ones, ident = tensors(ctx, [("gains", [P, 6, KT], F32), ("ones", [P, P], F32), ("ident", [P, P], F32)])
        pscale, m8, dskip, edge, kcol, eye = tensors(ctx, [
            ("pscale", [P, 4], F32), ("m8", [P, COLS], F32), ("dskip", [HG, G], F32),
            ("edge", [P, 4, 2, PAD], F32), ("kcol", [P, 2], F32), ("eye", [HG, HG], F32)])
        stat, tick = tensors(ctx, [("stat", [P, 4, 4], F32), ("tick", [P, 2], F32)])
        with ExitStack() as v:
            prep = tensors(v, [("prep", [P, 2 * KT * L], F32)])[0]
        ua_hi, ua_lo = tensors(ctx, [("ua_hi", [P, KT, L], F32R), ("ua_lo", [P, KT, L], F32R)])
        with ExitStack() as v:
            mem_t, mem_w, mn_hi, mn_lo, kv_hi, kv_lo = tensors(v, [
                ("mem_t", [P, KT, N_MEM], F32), ("mem_w", [P, KT, N_MEM], F32),
                ("mn_hi", [P, KT, N_MEM], F32R), ("mn_lo", [P, KT, N_MEM], F32R),
                ("kv_hi", [P, 2, KT * N_MEM], F32R), ("kv_lo", [P, 2, KT * N_MEM], F32R)])
        with ExitStack() as v:
            act_hi, act_lo, f_gate, f_silu, f_up, f_act = tensors(v, [
                ("act_hi", [P, 2, 2, L], F32R), ("act_lo", [P, 2, 2, L], F32R),
                ("f_gate", [P, L], F32), ("f_silu", [P, L], F32), ("f_up", [P, L], F32), ("f_act", [P, L], F32)])
        with ExitStack() as v:
            mx_lowest, mx_v, mx_a, mx_b = tensors(v, [
                ("mx_pooled", [P, 2, 2, L], F32R), ("mx_v", [P, L + 2 * PAD], F32),
                ("mx_a", [P, L + 2 * PAD], F32), ("mx_b", [P, L + 2 * PAD], F32)])
        pooled = mx_lowest
        with ExitStack() as v:
            merged, mixed_hi, mixed_lo = tensors(v, [
                ("merged", [P, KT, L], F32), ("mixed_hi", [P, 4, L], F32R), ("mixed_lo", [P, 4, L], F32R)])
        with ExitStack() as v:
            merged_again, z_a, z_b, z_c, z_d = tensors(v, [
                ("merged_again", [P, KT, L], F32), ("z_a", [P, 2, L], F32), ("z_b", [P, L], F32),
                ("z_c", [P, L], F32), ("z_d", [P, L], F32)])
        ub_hi, ub_lo = tensors(ctx, [("ub_hi", [P, KT, L], F32R), ("ub_lo", [P, KT, L], F32R)])
        with ExitStack() as v:
            pw_raw, pw_hi, pw_lo, u_t = tensors(v, [
                ("pw_raw", [P, 4, P], F32), ("pw_hi", [P, 4, P], F32R), ("pw_lo", [P, 4, P], F32R),
                ("u_t", [P, G, NC], F32)])
            with ExitStack() as w:
                s_perm = tensors(w, [("s_perm", [P, 2, T, NC], F32)])[0]
            e_m, f_m, m_m, tab, sw, st_, sx, y_t = tensors(v, [
                ("e_m", [P, 2, 2, P], F32), ("f_m", [P, 2, 2, P], F32), ("m_m", [P, 2, P], F32),
                ("tab", [P, 2, 2, NC], F32), ("sw", [P, 2, 2, NC], F32), ("st_", [P, 2, 2, NC], F32),
                ("sx", [P, 2, 2, NC + 1], F32), ("y_t", [P, 2, 2, NC], F32)])
        with ExitStack() as v:
            y_in, y_g, y_hi, y_lo = tensors(v, [
                ("y_in", [P, 2, T, NC], F32), ("y_g", [P, 2, L], F32),
                ("y_hi", [P, 2, L], F32R), ("y_lo", [P, 2, L], F32R)])
        with ExitStack() as v:
            k_hi, k_lo, v_hi, v_lo, pt_hi, pt_lo, prob = tensors(v, [
                ("k_hi", [P, 2, 2, N_MEM], F32R), ("k_lo", [P, 2, 2, N_MEM], F32R),
                ("v_hi", [P, 2, 2, HD], F32R), ("v_lo", [P, 2, 2, HD], F32R),
                ("pt_hi", [P, 2, HALF], F32R), ("pt_lo", [P, 2, HALF], F32R),
                ("prob", [P, 2, 4, N_MEM], F32)])
        h = tensors(ctx, [("h", [P, KT, L], F32)])[0]
        ps = [ctx.enter_context(nc.psum_tensor(f"ps{i}", [P, 2, HALF], F32)) for i in range(4)]

        def scratch(name, shape, dt=F32):
            return nc.dram_tensor(name, shape, dt).ap()

        d_kv_hi, d_kv_lo = (scratch(n, (2, P, KT * N_MEM)) for n in ("d_kv_hi", "d_kv_lo"))
        d_e, d_f = scratch("d_e", (P, 2, 2, G * S)), scratch("d_f", (P, 2, COLS, (T + 1) * HG))
        d_tab, d_k = scratch("d_tab", (P, 2, COLS, NC)), scratch("d_k", (HG, G, DIAGS * HG))
        d_m, d_s, d_y = scratch("d_m", (P, G, P)), scratch("d_s", (T, G * HG, NC)), scratch("d_y", (P, G, NC))
        d_h = scratch("d_h", (KT, P, L))

        raw_landed = [sem(f"raw_landed{i}") for i in range(RAW)]
        s_w_hi, s_w_split, s_w_used = sem("w_hi_written"), sem("w_split"), sem("w_used")
        s_prod, s_free = sem("product_done"), sem("psum_pair_free")
        s_dve, s_act = sem("dve_step"), None
        s_d2a, s_a2d, s_d2p = sem("dve_for_act"), sem("act_for_dve"), sem("dve_for_pe")
        s_const, s_mem, s_x, s_el, s_pl = (sem(n) for n in
                                           ("const_loaded", "mem_loaded", "x_loaded", "el_loaded", "pl_loaded"))
        s_estore, s_pstore, s_kstore, s_mstore, s_kvstore = (sem(n) for n in
            ("e_stored", "tab_f_stored", "k_stored", "m_stored", "kv_stored"))
        s_hspill, s_hload, s_pw, s_sst, s_uld = (sem(n) for n in
            ("h_spilled", "h_reloaded", "pool_w_loaded", "s_stored", "u_loaded"))
        s_step, s_yst, s_yld = sem("ssm_step_loaded"), [sem("y_stored0"), sem("y_stored1")], sem("y_loaded")
        s_kvld = [sem("kv_loaded0"), sem("kv_loaded1")]
        s_out, s_tick = sem("out_stored"), sem("tick_written")
        s_prob = sem("probabilities_normalised")
        block = ctx.enter_context(nc.Block())

        do_f1, do_mix, do_att, do_f2 = (c in stages for c in "1MA2")
        after_att = (ua_hi, ua_lo) if do_f2 else (None, None)
        after_mix = (ub_hi, ub_lo) if do_att else after_att
        u_hi, u_lo = (ub_hi, ub_lo) if stages[0] == "A" else (ua_hi, ua_lo)
        score_pair = {}
        units = len(stages_units(stages))
        def pc(k, w=D):
            return prep[:, k:k + w]

        EL = {n: pc(k * D) for k, n in enumerate(
            ("ar", "ai", "ld", "br", "bi", "dtar", "rr", "s", "c", "t1", "t2", "t3", "t4", "qr", "qi", "mag"))}
        PL = {n: pc(k * COLS, COLS) for k, n in enumerate(
            ("ar", "ai", "ld", "dtar", "rr", "s", "c", "t1", "t2", "t3", "t4", "qr", "qi", "mag", "r8"))}
        o = 512
        p_b = prep[:, o:o + 4 * 256].rearrange("p (q c x) -> p q c x", q=4, c=COLS)
        o += 1024
        p_bb = prep[:, o:o + 2 * 256].rearrange("p (q c x) -> p q c x", q=2, c=COLS)
        o += 512
        NE = COLS * (T + 1)
        kexp, k_ang, k_mag, k_s, k_c, k_t = (pc(o + q * NE, NE) for q in range(6))
        o += 6 * NE
        nidx = pc(o, NC)
        o += NC
        NCA = NE * HG
        ca = prep[:, o:o + 2 * NCA].rearrange("p (q c e x) -> p q c e x", q=2, c=COLS, e=T + 1)
        o += 2 * NCA
        ca_t = prep[:, o:o + NCA].rearrange("p (c e x) -> p c e x", c=COLS, e=T + 1)
        kp = prep[0:HG, o + NCA:o + NCA + G * DIAGS * HG].rearrange("p (g d x) -> p g d x", g=G, d=DIAGS)
        assert o + NCA + G * DIAGS * HG <= 2 * KT * L
        NT = COLS * NC
        t_r, t_s, t_c = (pc(o + q * NT, NT) for q in range(3))
        assert o + 3 * NT <= 2 * KT * L
        kv = {"k": 0, "v": 1}

        @block.sync
        def _(sp):
            def load(u, slot):
                sp.dma_start(raw[:, slot, :], a["weights"][u]).then_inc(raw_landed[slot], 16)

            for u in range(RAW):
                load(u, u)
            with sp.Fori(0, (units - RAW) // RAW) as i:
                for j in range(RAW):
                    sp.wait_ge(s_w_split, i * RAW + j + 1)
                    load(i * RAW + (RAW + j), j)

        @block.gpsimd
        def _(pool):
            def split(u, k, slot, wait_used=True):
                pool.wait_ge(raw_landed[k % RAW], 16 * (k // RAW + 1) if u is None else (u * (16 // RAW) + 16 * (k // RAW + 1)))
                if wait_used:
                    pool.wait_ge(s_w_used, k - RING + 1 if u is None else u + (k - RING + 1))
                if u is not None:
                    nc.gpsimd.tensor_tensor(tick[:, 1:2], tick[:, 0:1], tick[:, 0:1], op=ALU.add)
                hi, lo = w_hi[:, slot].rearrange("p k c -> p (k c)"), w_lo[:, slot].rearrange("p k c -> p (k c)")
                nc.gpsimd.tensor_scalar(hi, raw[:, k % RAW, :], 1.0, 0.0, ALU.mult, ALU.add).then_inc(s_w_hi, 1)
                pool.wait_ge(s_w_hi, k + 1 if u is None else u + (k + 1))
                nc.gpsimd.tensor_tensor(lo, raw[:, k % RAW, :], hi.bitcast(F32), op=ALU.subtract).then_inc(s_w_split, 1)

            body = RING * RAW
            nc.gpsimd.memset(tick[:], 0.0).then_inc(s_tick, 1)
            pool.wait_ge(s_tick, 1)
            for k in range(body):
                split(None, k, k % RING, k >= RING)
            trips = (units - body) // body
            with pool.Fori(0, trips) as i:
                for j in range(body):
                    split(i * body, body + j, j % RING)
            for k in range(body * (trips + 1), units):
                split(None, k, k % RING)

        @block.tensor
        def _(pe):
            unit, used, prod = Tally(s_w_split), Tally(s_w_used), Tally(s_prod)
            free, ready = Tally(s_free), Tally(s_d2p)
            all_tallies = (unit, used, prod, free, ready)
            owed = [0]

            def mm(out, lhsT, rhs, start, stop, done=False):
                ins = nc.tensor.matmul(out, lhsT, rhs, start=start, stop=stop)
                if done:
                    prod.add()
                    ins.then_inc(s_prod, 1)
                elif owed[0]:
                    owed[0] -= 1
                    used.add()
                    ins.then_inc(s_w_used, 1)
                return ins

            def take_unit():
                pe.wait_ge(s_w_split, unit.add())
                return (unit.n - 1) % RING

            def take_pair():
                k = prod.n + taken[0]
                if k >= 4:
                    pe.wait_ge(s_free, prod.at(4 - 1 - taken[0]))
                return ps[k % 4]
            taken = [0]

            def wait_dve():
                pe.wait_ge(s_d2p, ready.add())

            def three(out, whi, wlo, xhi, xlo, first, last, cols, done=False):
                for c, (o_c, x_c) in enumerate(cols):
                    mm(o_c(out), whi, x_c(xhi), first, False)
                    mm(o_c(out), whi, x_c(xlo), False, False)
                for c, (o_c, x_c) in enumerate(cols):
                    mm(o_c(out), wlo, x_c(xhi), False, last, done and c == len(cols) - 1)

            HALVES = [(lambda t, c=c: t[:, c, :], lambda x, c=c: x[:, c * HALF:(c + 1) * HALF]) for c in range(2)]

            def product(whi, wlo, xhi, xlo, tiles, t0=0, each=None):
                pair = take_pair()
                for k in range(tiles):
                    if each:
                        each()
                    three(pair, whi[:, t0 + k], wlo[:, t0 + k], xhi[:, k], xlo[:, k], k == 0, k == tiles - 1,
                          HALVES, done=(k == tiles - 1))

            def unit_product(xhi, xlo, each=None):
                s = take_unit()
                product(w_hi[:, s], w_lo[:, s], xhi, xlo, KT, each=each)
                owed[0] += 1

            def norm_product(x=None, width=L):
                pair = take_pair()
                wait_dve()
                n = max(1, width // HALF)
                w = width // n
                for c in range(n):
                    mm(pair[:, c, 0:w], ones[:], acc[:, c * w:(c + 1) * w], True, True, done=(c == n - 1))

            if do_att:
                norm_product(width=N_MEM)
                wait_dve()
                one = [(lambda t: t[:, 0, 0:N_MEM], lambda x: x)]
                for m in range(KT):
                    s = take_unit()
                    pair = take_pair()
                    for k in range(KT):
                        three(pair, w_hi[:, s, k], w_lo[:, s, k], mn_hi[:, k], mn_lo[:, k], k == 0, k == KT - 1,
                              one, done=(k == KT - 1))
                    owed[0] += 1
                pairs = []
                for t in range(2):
                    taken[0] = t
                    pairs.append(take_pair())
                taken[0] = 0
                for k in range(KT):
                    s = take_unit()
                    wh, wl = (w[:, s].rearrange("p k c -> p (k c)") for w in (w_hi, w_lo))
                    for t in range(2):
                        rows = slice(t * P, (t + 1) * P)
                        for c in range(2):
                            cs = slice(c * HALF, (c + 1) * HALF)
                            mm(pairs[t][:, c], mn_hi[:, k, rows], wh[:, cs], k == 0, False)
                            mm(pairs[t][:, c], mn_hi[:, k, rows], wl[:, cs], False, False)
                        for c in range(2):
                            cs = slice(c * HALF, (c + 1) * HALF)
                            mm(pairs[t][:, c], mn_lo[:, k, rows], wh[:, cs], False, k == KT - 1,
                               done=(k == KT - 1 and c == 1))
                    owed[0] += 1
            if do_mix:
                wait_dve()
                for dr in range(2):
                    for gh in range(2):
                        pair = take_pair()
                        for g8 in range(8):
                            g = gh * 8 + g8
                            rows = slice((g % 2) * S, (g % 2 + 1) * S)
                            col = dr * PAIRS + g // 2
                            for q in range(2):
                                mm(pair[0:HG, g8 % 2, (g8 // 2) * P:(g8 // 2 + 1) * P], p_bb[rows, q, col, :],
                                   ca[rows, q, col, dr:dr + T, :].rearrange("p e x -> p (e x)"), q == 0, q == 1,
                                   done=(q == 1 and g8 == 7))

            def ffn(xhi, xlo):
                def down(b, act_ready=True):
                    sl = [take_unit(), take_unit()]
                    for m in range(KT):
                        pair = take_pair()
                        for k in range(2):
                            if m == 0:
                                wait_dve()
                            if m == KT - 1 and k == 1:
                                owed[0] += 1
                            three(pair, w_hi[:, sl[k], m], w_lo[:, sl[k], m], act_hi[:, b, k], act_lo[:, b, k],
                                  k == 0, k == 1, HALVES, done=(k == 1))
                    owed[0] += 1

                unit_product(xhi, xlo, each=wait_dve)
                norm_product()
                for _ in range(3):
                    unit_product(xhi, xlo)
                with pe.Fori(0, FT // 4) as i:
                    for t, stride in zip(all_tallies, (12, 12, 24, 0, 4)):
                        t.enter(i, stride)
                    for b in range(2):
                        for _ in range(4):
                            unit_product(xhi, xlo)
                        down(b)
                    for t in all_tallies:
                        t.leave(FT // 4)
                down(0)

            if do_f1:
                ffn(ua_hi, ua_lo)
            if do_mix:
                unit_product(ua_hi, ua_lo, each=wait_dve)
                norm_product()
                for _ in range(3):
                    unit_product(ua_hi, ua_lo)

                def pool_mix(g):
                    pair = take_pair()
                    wait_dve()
                    three(pair, pw_hi[:, g], pw_lo[:, g], pooled[:, g % 2, 0], pooled[:, g % 2, 1], True, True,
                          HALVES, done=True)

                def ssm_states(q):
                    pair = take_pair()
                    wait_dve()
                    for ri in range(2):
                        for dr in range(2):
                            for gg in range(2):
                                rhs = u_t[:, 2 * q + gg, :] if dr == 0 else u_t[:, 2 * q + gg, ::-1]
                                mm(pair[gg * S:(gg + 1) * S, ri, dr * NC:(dr + 1) * NC], e_m[:, dr, ri, gg * S:(gg + 1) * S],
                                   rhs, True, True, done=(ri == 1 and dr == 1 and gg == 1))

                def ssm_out(q):
                    pair = take_pair()
                    wait_dve()
                    for gg in range(2):
                        rows = slice(gg * S, (gg + 1) * S)
                        out = pair[:, gg, 0:NC]
                        mm(out, m_m[:, gg, :], u_t[:, 2 * q + gg, :], True, False)
                        for dr in range(2):
                            for ri in range(2):
                                x = sx[rows, ri, dr, 0:NC] if dr == 0 else sx[rows, ri, dr, 0:NC][:, ::-1]
                                mm(out, f_m[rows, ri, dr, :], x, False, dr == 1 and ri == 1,
                                   done=(dr == 1 and ri == 1 and gg == 1))

                pool_mix(0)
                unit_product(ua_hi, ua_lo)
                pool_mix(1)
                unit_product(ua_hi, ua_lo)
                pool_mix(2)
                pool_mix(3)
                for m in range(KT):
                    ssm_states(m)
                    unit_product(ua_hi, ua_lo)
                    ssm_out(m)
                wait_dve()
                for j in range(KT // 2):
                    s = take_unit()
                    for m2 in range(2):
                        product(w_hi[:, s], w_lo[:, s], mixed_hi, mixed_lo, 4, t0=4 * m2)
                    owed[0] += 1
                for j in range(KT // 2):
                    unit_product(ua_hi, ua_lo)
                    unit_product(ua_hi, ua_lo)
                    if j == 0:
                        wait_dve()
                    s = take_unit()
                    for m2 in range(2):
                        for vg in range(2):
                            product(w_hi[:, s], w_lo[:, s], y_hi, y_lo, 2, t0=4 * m2 + 2 * vg)
                    owed[0] += 1
                for m in range(KT):
                    unit_product(ua_hi, ua_lo, each=wait_dve if m == 0 else None)
            if do_att:
                unit_product(ub_hi, ub_lo, each=wait_dve)
                norm_product()
                for m in range(1, KT):
                    unit_product(ub_hi, ub_lo)

                def scores(j):
                    hd, c = j // 2, j % 2
                    score_pair[j] = prod.n % 4
                    pair = take_pair()
                    if j == 0:
                        wait_dve()
                    if c == 0:
                        pe.wait_ge(s_kvld[hd % 2], 64 * (hd // 2 + 1))
                    for t in range(4):
                        cols = slice(c * HALF + t * P, c * HALF + (t + 1) * P)
                        out = pair[:, t // 2, (t % 2) * N_MEM:(t % 2 + 1) * N_MEM]
                        for d in range(2):
                            qh, ql = ua_hi[:, 2 * hd + d, cols], ua_lo[:, 2 * hd + d, cols]
                            mm(out, qh, k_hi[:, hd % 2, d], d == 0, False)
                            mm(out, qh, k_lo[:, hd % 2, d], False, False)
                            mm(out, ql, k_hi[:, hd % 2, d], False, d == 1, done=(d == 1 and t == 3))

                def turn(j):
                    pair = take_pair()
                    pe.wait_ge(s_prob, j + 1)
                    for t in range(4):
                        for mt in range(2):
                            ins = nc.tensor.transpose(pair[:, mt, t * P:(t + 1) * P],
                                                      prob[:, j % 2, t, mt * P:(mt + 1) * P], ident[:])
                    prod.add()
                    ins.then_inc(s_prod, 1)

                def attend(j):
                    hd = j // 2
                    pair = take_pair()
                    wait_dve()
                    for d in range(2):
                        for mt in range(2):
                            vh, vl = (x[:, hd % 2, mt, d * P:(d + 1) * P] for x in (v_hi, v_lo))
                            mm(pair[:, d], vh, pt_hi[:, mt], mt == 0, False)
                            mm(pair[:, d], vh, pt_lo[:, mt], False, False)
                            mm(pair[:, d], vl, pt_hi[:, mt], False, mt == 1, done=(mt == 1 and d == 1))

                scores(0)
                scores(1)
                for j in range(2 * HEADS):
                    turn(j)
                    if j + 2 < 2 * HEADS:
                        scores(j + 2)
                    attend(j)
                wait_dve()
                for m in range(KT):
                    unit_product(ub_hi, ub_lo)
            if do_f2:
                ffn(ua_hi, ua_lo)
            norm_product()
            assert unit.n == units, (unit.n, units)

        @block.scalar
        def _(act):
            from_dve, to_dve = Tally(s_d2a), Tally(s_a2d)
            kv_loads = [0, 0]

            def wait_dve():
                act.wait_ge(s_d2a, from_dve.add())

            def run(out, in_, func, last=True, **kw):
                ins = nc.scalar.activation(out, in_, func, **kw)
                if last:
                    to_dve.add()
                    ins.then_inc(s_a2d, 1)
                return ins

            def one(out, in_, func, **kw):
                wait_dve()
                run(out, in_, func, **kw)

            def load(dst, src, s):
                act.dma_start(dst, src).then_inc(s, 16)

            load(mem_t[:], a["mem"], s_mem)
            for dst, n in ((gains, "gains"), (ones, "ones"), (ident, "ident"), (pscale, "pool_scale"), (dskip, "dskip"),
                           (edge, "edge"), (kcol, "kcol"), (eye, "eye")):
                load(dst[:], a[n], s_const)
            if do_mix:
                def load_el(dr):
                    for k, n in enumerate(("ar", "ai", "ld")):
                        load(EL[n], a["el_a"][dr, k], s_el)
                    for k, n in enumerate(("br", "bi")):
                        load(EL[n], a["el_b"][dr, k], s_el)
                load_el(0)
            for k in range(KT):
                load(h[:, k], a["x"][k], s_x)

            def trig(r, s, c):
                wait_dve()
                run(s, r, ACT.Sin, last=False)
                run(c, r, ACT.Sin, scale=0.5)

            if do_att:
                one(mem_w[:].rearrange("p k t -> p (k t)"), mem_t[:].rearrange("p k t -> p (k t)"), ACT.Square)
                one(sq[:, 0:N_MEM], acc[:, 0:N_MEM], ACT.Sqrt)
            if do_mix:
                for dr in range(2):
                    if dr:
                        wait_dve()
                        load_el(dr)
                    one(EL["t1"], EL["ld"], ACT.Exp)
                    one(EL["mag"], EL["dtar"], ACT.Exp)
                    trig(EL["rr"], EL["s"], EL["c"])
                    wait_dve()
                    run(EL["mag"], EL["dtar"], ACT.Exp, scale=kcol[:, dr:dr + 1])
                    trig(EL["t1"], EL["s"], EL["c"])
                    wait_dve()
                    for ri, n in enumerate(("t3", "t4")):
                        load(d_e[:, dr, ri, :], EL[n], s_estore)
                act.wait_ge(s_estore, 64)
                for k, n in enumerate(("ar", "ai", "ld")):
                    load(PL[n], a["pl_a"][k], s_pl)
                load(prep[:, 512:1536], a["pl_bc"], s_pl)
                load(kexp, a["kexp"], s_pl)
                load(nidx, a["nidx"], s_pl)
                one(PL["t1"], PL["ld"], ACT.Exp)
                one(PL["mag"], PL["dtar"], ACT.Exp)
                trig(PL["rr"], PL["s"], PL["c"])
                wait_dve()
                run(m8[:], PL["dtar"], ACT.Exp, scale=float(T))
                trig(t_r, t_s, t_c)
                wait_dve()
                for k, t in enumerate((t_c, t_s)):
                    load(d_tab[:, k].rearrange("p c n -> p (c n)"), t, s_pstore)
                one(k_mag, k_mag, ACT.Exp)
                trig(k_ang, k_s, k_c)
                wait_dve()
                load(d_f, ca[:].rearrange("p q c e x -> p q c (e x)"), s_pstore)
                wait_dve()
                load(d_k, kp[:].rearrange("p g d x -> p g (d x)"), s_kstore)
                act.wait_ge(s_kstore, 16)
                act.wait_ge(s_pstore, 48)
                for i in range(T):
                    load(d_m[HG * i:HG * (i + 1)], d_k[:, :, (T - 1 - i) * HG:(T - 1 - i) * HG + P], s_mstore)
            if do_att:
                wait_dve()
                for d, t in ((d_kv_hi, kv_hi), (d_kv_lo, kv_lo)):
                    load(d.rearrange("q p n -> p q n"), t[:].bitcast(F32), s_kvstore)

            def boundary(m, dst, gi, split=True):
                wait_dve()
                if split:
                    run(dst[:, m], h[:, m], ACT.Copy, scale=gains[:, gi, m:m + 1])
                run(acc[:] if m == 0 else sq[:], h[:, m], ACT.Square)

            def root():
                one(sq[:], acc[:], ACT.Sqrt)

            def ffn(next_dst, gi):
                root()

                def hidden(b, t):
                    one(f_silu[:], f_gate[:], ACT.Silu)
                    one(act_hi[:, b, t], f_act[:], ACT.Copy)
                for t in range(2):
                    hidden(0, t)
                with act.Fori(0, FT // 4) as i:
                    from_dve.enter(i, 8)
                    to_dve.enter(i, 8)
                    for b in range(2):
                        for t in range(2):
                            hidden(1 - b, t)
                    from_dve.leave(FT // 4)
                    to_dve.leave(FT // 4)
                for m in range(KT):
                    boundary(m, next_dst, gi, next_dst is not None)

            for m in range(KT):
                boundary(m, u_hi, 0)
            if do_f1:
                ffn(ua_hi if (do_mix or do_f2) else None, 1)
            if do_mix:
                for m in range(KT):
                    load(d_h[m], h[:, m], s_hspill)
                root()
                act.wait_ge(s_hspill, 16 * KT)
                load(pw_raw[:], a["pool_w"], s_pw)
                for t in range(2):
                    wait_dve()
                    load(d_s[:, t * P:(t + 1) * P, :].rearrange("i c n -> c i n"), s_perm[:, t], s_sst)
                    if t == 1:
                        act.wait_ge(s_sst, 32)
                        for i in range(T):
                            load(u_t[HG * i:HG * (i + 1)], d_s[i].rearrange("(g c) n -> c g n", c=HG), s_uld)
                act.wait_ge(s_estore, 64)
                act.wait_ge(s_pstore, 48)
                act.wait_ge(s_mstore, 16 * T)

                def load_step(q):
                    load(e_m[:], d_e[:, :, :, q * P:(q + 1) * P], s_step)
                    load(m_m[:], d_m[:, 2 * q:2 * q + 2, :], s_step)
                    for dr in range(2):
                        load(f_m[:, :, dr], d_f[:, :, dr * PAIRS + q, (1 - dr) * HG:(1 - dr) * HG + P], s_step)
                        load(tab[:, :, dr], d_tab[:, :, dr * PAIRS + q, :], s_step)

                for q in range(PAIRS):
                    wait_dve()
                    load_step(q)
                    one(merged[:, KT - 1 - q], merged[:, KT - 1 - q], ACT.Sigmoid)
                    wait_dve()
                    load(d_y[:, 2 * q:2 * q + 2, :], y_t[:, q % 2], s_yst[q % 2])
                for k in range(2):
                    act.wait_ge(s_yst[k], 16 * PAIRS // 2)
                for g in range(G):
                    load(y_in[HG * (g % 8):HG * (g % 8 + 1), g // 8],
                         d_y[:, g, :].rearrange("(i c) n -> c i n", c=HG), s_yld)
                act.wait_ge(s_yld, 16 * G)
                for t in range(2):
                    run(y_g[:, t].rearrange("p (n i) -> p i n", i=T), y_in[:, t], ACT.Gelu_apprx_tanh, last=(t == 1))
                for j in range(KT // 2):
                    for m2 in range(2):
                        one(z_a[:, m2], z_a[:, m2], ACT.Sigmoid)
                    for m2 in range(2):
                        one(z_c[:], z_b[:], ACT.Sigmoid)
                wait_dve()
                for m in range(KT):
                    load(h[:, m], d_h[m], s_hload)
                for m in range(KT):
                    run(ua_hi[:, m], merged[:, m], ACT.Copy)
                for m in range(KT):
                    boundary(m, after_mix[0], 2, after_mix[0] is not None)
            if do_att:
                for m in range(KT):
                    load(d_h[m], h[:, m], s_hspill)
                root()
                act.wait_ge(s_hspill, 16 * KT * (2 if do_mix else 1))
                act.wait_ge(s_kvstore, 32)

                def load_kv(hd):
                    for src, kd, vd in ((d_kv_hi, k_hi, v_hi), (d_kv_lo, k_lo, v_lo)):
                        load(kd[:, hd % 2].bitcast(F32), src[0].rearrange("p (m t) -> p m t", m=KT)[:, 2 * hd:2 * hd + 2], s_kvld[hd % 2])
                        load(vd[:, hd % 2].bitcast(F32), src[1].rearrange("p (m d) -> p m d", m=2)[:, :, hd * HD:(hd + 1) * HD],
                             s_kvld[hd % 2])
                load_kv(0)
                load_kv(1)
                for m in range(KT):
                    one(ua_hi[:, m], sq[:], ACT.Copy)

                def softmax(j):
                    wait_dve()
                    for t in range(4):
                        run(prob[:, j % 2, t], ps[score_pair[j]][:, t // 2, (t % 2) * N_MEM:(t % 2 + 1) * N_MEM], ACT.Exp,
                            last=(t == 3), bias=stat[:, 1, t:t + 1], scale=HD ** -0.5, accum_out=stat[:, 2, t:t + 1])
                softmax(0)
                softmax(1)
                for j in range(2 * HEADS):
                    if j + 2 < 2 * HEADS:
                        softmax(j + 2)
                    if j % 2 == 1:
                        wait_dve()
                        if j // 2 + 2 < HEADS:
                            load_kv(j // 2 + 2)
                for m in range(KT):
                    load(h[:, m], d_h[m], s_hload)
                for m in range(KT):
                    boundary(m, after_att[0], 4, do_f2)
            if do_f2:
                ffn(None, 0)
            root()
            for m in range(KT):
                wait_dve()
                load(a["out"][m], h[:, m], s_out)
            act.wait_ge(s_out, 16 * KT)

        @block.vector
        def _(dve):
            step, prod, free = Tally(s_dve), Tally(s_prod), Tally(s_free)
            to_act, from_act, to_pe = Tally(s_d2a), Tally(s_a2d), Tally(s_d2p)
            all_tallies = (step, prod, free, to_act, from_act, to_pe)
            v = nc.vector

            def link(ins, tally=step):
                tally.add()
                ins.then_inc(tally.sem, 1)
                dve.wait_ge(tally.sem, tally.at())

            def wait_act():
                dve.wait_ge(s_a2d, from_act.add())

            def pair_of():
                return ps[(prod.n - 1) % 4]

            def wait_product():
                dve.wait_ge(s_prod, prod.add())
                return pair_of()[:].rearrange("p c n -> p (c n)")

            def tt(out, x, y, op=ALU.mult, tally=step):
                link(v.tensor_tensor(out, x, y, op), tally)

            def ts(out, x, s1, s2=None, op0=ALU.mult, op1=None, tally=step):
                if op1 is None:
                    link(v.tensor_scalar(out, x, s1, None, op0), tally)
                else:
                    link(v.tensor_scalar(out, x, s1, s2, op0, op1), tally)

            def stt(out, x, s, y, op0, op1, tally=step):
                link(v.scalar_tensor_tensor(out=out, in0=x, scalar=s, in1=y, op0=op0, op1=op1), tally)

            def cp(out, x, tally=step):
                link(v.tensor_copy(out, x), tally)

            def rounded(r, ang, k):
                ts(k, ang, INV_2PI, ROUND, ALU.mult, ALU.add)
                ts(k, k, ROUND, None, ALU.subtract)
                stt(r, k, -TWO_PI_HI, ang, ALU.mult, ALU.add)
                stt(r, k, -TWO_PI_LO, r, ALU.mult, ALU.add)
                ts(r, r, PI_IN, -PI_IN, ALU.min, ALU.max, tally=to_act)

            def cosine(c):
                wait_act()
                tt(c, c, c)
                ts(c, c, -2.0, 1.0, ALU.mult, ALU.add)

            def root_factor(w, tally=free):
                pair = wait_product()
                ts(acc[:, 0:w], pair[:, 0:w], 1.0 / D, EPS, ALU.mult, ALU.add, tally=to_act)
                wait_act()
                link(v.reciprocal(rn[:, 0:w], sq[:, 0:w]))
                tt(sq[:, 0:w], rn[:, 0:w], rn[:, 0:w])
                tt(sq[:, 0:w], sq[:, 0:w], acc[:, 0:w])
                ts(sq[:, 0:w], sq[:, 0:w], -0.5, 1.5, ALU.mult, ALU.add)
                tt(rn[:, 0:w], rn[:, 0:w], sq[:, 0:w], tally=tally)

            def discretise(q, rows=None):
                wait_act()
                tt(q["dtar"], q["t1"], q["ar"], tally=to_act)
                tt(q["t2"], q["t1"], q["ai"])
                wait_act()
                rounded(q["rr"], q["t2"], q["t3"])
                tt(q["t1"], q["ar"], q["ar"])
                tt(q["t2"], q["ai"], q["ai"])
                tt(q["t1"], q["t1"], q["t2"], ALU.add)
                link(v.reciprocal(q["t4"], q["t1"]))
                cosine(q["c"])
                tt(q["t1"], q["mag"], q["c"])
                ts(q["t1"], q["t1"], 1.0, None, ALU.subtract)
                tt(q["t2"], q["mag"], q["s"])
                tt(q["qr"], q["t1"], q["ar"])
                tt(q["t3"], q["t2"], q["ai"])
                tt(q["qr"], q["qr"], q["t3"], ALU.add)
                tt(q["qr"], q["qr"], q["t4"])
                tt(q["qi"], q["t2"], q["ar"])
                tt(q["t3"], q["t1"], q["ai"])
                tt(q["qi"], q["qi"], q["t3"], ALU.subtract)
                tt(q["qi"], q["qi"], q["t4"])

            def complex_mult(re, im, ar, ai, br, bi, tmp, neg_im=False, tally=step):
                tt(re, ar, br)
                tt(tmp, ai, bi)
                tt(re, re, tmp, ALU.subtract)
                tt(im, ar, bi)
                tt(tmp, ai, br)
                if neg_im:
                    stt(im, im, -1.0, tmp, ALU.mult, ALU.subtract, tally=tally)
                else:
                    tt(im, im, tmp, ALU.add, tally=tally)

            def first(tally=to_act):
                link(v.memset(stat[:, 3, 0:1], 0.0), tally)

            dve.wait_ge(s_const, 16 * 8)
            if do_att:
                dve.wait_ge(s_mem, 16)
                first()
                wait_act()
                link(v.tensor_reduce(acc[:, 0:N_MEM], mem_w[:].rearrange("p k t -> p t k"), AX, ALU.add), to_pe)
                root_factor(N_MEM)
                for k in range(KT):
                    stt(mem_w[:, k], mem_t[:, k], gains[:, 3, k:k + 1], rn[:, 0:N_MEM], ALU.mult, ALU.mult)
                cp(mn_hi[:], mem_w[:])
                tt(mn_lo[:], mem_w[:], mn_hi[:].bitcast(F32), ALU.subtract, tally=to_pe)
            kv_left = list(range(KT + 2)) if do_att else []

            def store_kv():
                if not kv_left:
                    return
                m = kv_left.pop(0)
                pair = wait_product()
                if m < KT:
                    hi, lo, src = kv_hi[:, 0, m * N_MEM:(m + 1) * N_MEM], kv_lo[:, 0, m * N_MEM:(m + 1) * N_MEM], pair[:, 0:N_MEM]
                else:
                    n = m - KT
                    hi, lo, src = kv_hi[:, 1, n * D:(n + 1) * D], kv_lo[:, 1, n * D:(n + 1) * D], pair
                cp(hi, src)
                tt(lo, src, hi.bitcast(F32), ALU.subtract, tally=free)

            if do_mix:
                for dr in range(2):
                    q = EL
                    if dr:
                        first()
                        dve.wait_ge(s_estore, 32)
                    dve.wait_ge(s_el, 80 * (dr + 1))
                    first()
                    store_kv()
                    discretise(q)
                    store_kv()
                    complex_mult(q["t2"], q["t3"], q["qr"], q["qi"], q["br"], q["bi"], q["t4"])
                    ts(q["t4"], q["rr"], kcol[:, dr:dr + 1], tally=to_act)
                    wait_act()
                    store_kv()
                    rounded(q["t1"], q["t4"], q["qr"])
                    cosine(q["c"])
                    tt(q["s"], q["s"], q["mag"])
                    tt(q["c"], q["c"], q["mag"])
                    tt(q["qr"], q["t2"], q["c"])
                    tt(q["qi"], q["t3"], q["s"])
                    tt(q["qr"], q["qr"], q["qi"], ALU.subtract)
                    tt(q["qi"], q["t2"], q["s"])
                    tt(q["t4"], q["t3"], q["c"])
                    cp(q["t3"], q["qr"])
                    tt(q["t4"], q["t4"], q["qi"], ALU.add, tally=to_act)
                    store_kv()
                q = PL
                dve.wait_ge(s_pl, 96)
                first()
                discretise(q)
                store_kv()
                bro = lambda t: t.unsqueeze(2).to_broadcast([P, COLS, HG])
                complex_mult(p_bb[:, 0], p_bb[:, 1], bro(q["qr"]), bro(q["qi"]), p_b[:, 0], p_b[:, 1],
                             prep[:, o:o + COLS * HG].rearrange("p (c x) -> p c x", c=COLS))
                ts(q["t4"], q["rr"], float(T), None)
                rounded8 = q["r8"]
                ts(q["t3"], q["t4"], INV_2PI, ROUND, ALU.mult, ALU.add)
                ts(q["t3"], q["t3"], ROUND, None, ALU.subtract)
                stt(rounded8, q["t3"], -TWO_PI_HI, q["t4"], ALU.mult, ALU.add)
                stt(rounded8, q["t3"], -TWO_PI_LO, rounded8, ALU.mult, ALU.add, tally=to_act)
                wait_act()
                r3 = lambda t: t.rearrange("p (c n) -> p c n", c=COLS)
                tt(r3(t_c), rounded8.unsqueeze(2).to_broadcast([P, COLS, NC]), nidx.unsqueeze(1).to_broadcast([P, COLS, NC]))
                rounded(t_r, t_c, t_s)
                store_kv()
                cosine(t_c)
                first()
                e3 = lambda t: t.rearrange("p (c e) -> p c e", c=COLS)
                be = lambda t: t.unsqueeze(2).to_broadcast([P, COLS, T + 1])
                tt(e3(k_mag), e3(kexp), be(q["dtar"]), tally=to_act)
                tt(e3(k_t), e3(kexp), be(q["rr"]))
                wait_act()
                rounded(k_ang, k_t, k_c)
                store_kv()
                cosine(k_c)
                tt(k_s, k_s, k_mag)
                tt(k_c, k_c, k_mag)
                dve.wait_ge(s_pstore, 32)
                w4 = lambda t: e3(t).unsqueeze(3).to_broadcast([P, COLS, T + 1, HG])
                c4 = lambda k: p_b[:, k].unsqueeze(2).to_broadcast([P, COLS, T + 1, HG])
                complex_mult(ca[:, 0], ca[:, 1], w4(k_c), w4(k_s), c4(2), c4(3), ca_t, neg_im=True, tally=to_act)
            while kv_left:
                store_kv()
            if do_mix:
                first(to_pe)
                for dr in range(2):
                    for gh in range(2):
                        wait_product()
                        pair = pair_of()[0:HG].rearrange("p c (g e x) -> p c g e x", g=4, e=T)
                        for c in range(2):
                            out, src = kp[:, gh * 8 + c:gh * 8 + 8:2], pair[:, c]
                            end = free if c else step
                            if dr == 0:
                                cp(out[:, :, T - 1:DIAGS], src, tally=end)
                            else:
                                cp(out[:, :, 0:T - 1], src[:, :, 0:T - 1])
                                tt(out[:, :, T - 1], out[:, :, T - 1], src[:, :, T - 1], ALU.add, tally=end)
                for g in range(G):
                    stt(kp[:, g, T - 1], eye[:], dskip[:, g:g + 1], kp[:, g, T - 1], ALU.mult, ALU.add,
                        tally=to_act if g == G - 1 else step)
            if do_att:
                first()

            def boundary(m, dst_hi, dst_lo, gi):
                if dst_hi is not None:
                    wait_act()
                    stt(dst_lo[:, m], h[:, m], gains[:, gi, m:m + 1], dst_hi[:, m].bitcast(F32),
                        ALU.mult, ALU.subtract, tally=to_pe)
                wait_act()
                if m:
                    tt(acc[:], acc[:], sq[:], ALU.add, tally=to_pe if m == KT - 1 else step)

            if do_att:
                dve.wait_ge(s_kvstore, 32)
            for m in range(KT):
                dve.wait_ge(s_x, 16 * KT)
                first()
                boundary(m, u_hi, u_lo, 0)

            def residual(m, coef):
                pair = wait_product()
                link(v.scalar_tensor_tensor(out=h[:, m], in0=pair, scalar=coef, in1=h[:, m], op0=ALU.mult, op1=ALU.add), free)

            def evacuate_after_norm(evac):
                prod.add()
                root_factor(L, tally=step)
                held = ps[(prod.n - 2) % 4][:].rearrange("p c n -> p (c n)")
                evac(held)
                first(free)

            def ffn(next_hi, next_lo, gi):
                def gate(pair):
                    tt(f_gate[:], pair, rn[:], tally=free)
                    first()

                def hidden(b, t, started=False):
                    if not started:
                        gate(wait_product())
                    pair = wait_product()
                    tt(f_up[:], pair, rn[:], tally=free)
                    wait_act()
                    tt(f_act[:], f_silu[:], f_up[:], tally=to_act)
                    wait_act()
                    tt(act_lo[:, b, t], f_act[:], act_hi[:, b, t].bitcast(F32), ALU.subtract, tally=to_pe)

                evacuate_after_norm(gate)
                hidden(0, 0, started=True)
                hidden(0, 1)
                with dve.Fori(0, FT // 4) as i:
                    for t, stride in zip(all_tallies, (0, 24, 24, 8, 8, 4)):
                        t.enter(i, stride)
                    for b in range(2):
                        for t in range(2):
                            hidden(1 - b, t)
                        for m in range(KT):
                            residual(m, 0.5)
                    for t in all_tallies:
                        t.leave(FT // 4)
                for m in range(KT):
                    residual(m, 0.5)
                    first()
                    boundary(m, next_hi, next_lo, gi)

            if do_f1:
                nx = (ua_hi, ua_lo) if (do_mix or do_f2) else (None, None)
                ffn(*nx, 1)
            if do_mix:
                def evac_s(t):
                    def go(pair):
                        if t == 0:
                            dve.wait_ge(s_hspill, 16 * KT)
                        tt(s_perm[:, t].rearrange("p i n -> p n i"), pair.rearrange("p (n i) -> p n i", i=T),
                           rn[:].rearrange("p (n i) -> p n i", i=T), tally=free)
                        first()
                    return go
                evacuate_after_norm(evac_s(0))
                evac_s(1)(wait_product())
                dve.wait_ge(s_pw, 16)
                cp(pw_hi[:], pw_raw[:])
                tt(pw_lo[:], pw_raw[:], pw_hi[:].bitcast(F32), ALU.subtract)
                for t in (mx_v, mx_a, mx_b):
                    link(v.memset(t[:], 0.0))

                def pool(g):
                    pair = wait_product()
                    w = WINDOWS[g]
                    tt(mx_v[:, PAD:PAD + L], pair, rn[:], tally=free)
                    n = L + 2 * PAD
                    tt(mx_a[:, 1:n], mx_v[:, 0:n - 1], mx_v[:, 1:n], ALU.add)
                    cur, nxt, size = mx_a, mx_b, 2
                    while size < w:
                        k = size // 2
                        tt(nxt[:, k:n - k], cur[:, 0:n - 2 * k], cur[:, 2 * k:n], ALU.add)
                        cur, nxt, size = nxt, cur, 2 * size
                    for side in range(2):
                        cols = slice(PAD, 2 * PAD) if side == 0 else slice(L, L + PAD)
                        tt(cur[:, cols], cur[:, cols], edge[:, g, side])
                    stt(nxt[:, PAD:PAD + L], cur[:, PAD:PAD + L], 1.0 / w, mx_v[:, PAD:PAD + L], ALU.mult, ALU.subtract)
                    hi, lo = pooled[:, g % 2, 0], pooled[:, g % 2, 1]
                    cp(hi, nxt[:, PAD:PAD + L])
                    tt(lo, nxt[:, PAD:PAD + L], hi.bitcast(F32), ALU.subtract, tally=to_pe)

                def pool_mixed(g):
                    pair = wait_product()
                    ts(mx_v2[:], pair, pscale[:, g:g + 1], tally=free)
                    cp(mixed_hi[:, g], mx_v2[:])
                    tt(mixed_lo[:, g], mx_v2[:], mixed_hi[:, g].bitcast(F32), ALU.subtract)
                mx_v2 = acc

                pool(0)
                pool(1)
                pool_mixed(0)
                pool(2)
                pool_mixed(1)
                pool(3)
                pool_mixed(2)
                pool_mixed(3)
                link(v.memset(sx[:], 0.0))
                dve.wait_ge(s_uld, 16 * T)
                for q in range(PAIRS):
                    first()
                    dve.wait_ge(s_step, 96 * (q + 1))
                    first(to_pe)
                    pair = wait_product()
                    re, im = (pair[:, k * HALF:k * HALF + 2 * NC].rearrange("p (d n) -> p d n", d=2) for k in range(2))
                    ct, sn = tab[:, 0], tab[:, 1]
                    tt(sw[:, 0], re, ct)
                    tt(st_[:, 0], im, sn)
                    tt(sw[:, 0], sw[:, 0], st_[:, 0], ALU.add)
                    tt(sw[:, 1], im, ct)
                    tt(st_[:, 0], re, sn, tally=free)
                    tt(sw[:, 1], sw[:, 1], st_[:, 0], ALU.subtract)
                    for dr in range(2):
                        mag = m8[:, dr * PAIRS + q:dr * PAIRS + q + 1].to_broadcast([P, NC])
                        for ri in range(2):
                            link(v.tensor_tensor_scan(st_[:, ri, dr], mag, sw[:, ri, dr], 0.0, ALU.mult, ALU.add))
                    tt(sw[:, 0], st_[:, 0], ct)
                    tt(sw[:, 1], st_[:, 1], sn)
                    tt(sx[:, 0, :, 1:], sw[:, 0], sw[:, 1], ALU.subtract)
                    tt(sw[:, 0], st_[:, 1], ct)
                    tt(sw[:, 1], st_[:, 0], sn)
                    tt(sx[:, 1, :, 1:], sw[:, 0], sw[:, 1], ALU.add, tally=to_pe)
                    pair = wait_product()
                    tt(merged[:, KT - 1 - q], pair, rn[:], tally=free)
                    first()
                    pair = wait_product()
                    if q >= 2:
                        dve.wait_ge(s_yst[q % 2], 16 * (q // 2))
                    cp(y_t[:, q % 2], pair.rearrange("p (g n) -> p g n", g=2)[:, :, 0:NC], tally=free)
                    first()
                    wait_act()
                first(to_pe)
                for m in range(KT):
                    pair = wait_product()
                    tt(merged[:, KT - 1 - m], merged[:, KT - 1 - m], pair, tally=free)
                wait_act()
                cp(y_hi[:], y_g[:])
                tt(y_lo[:], y_g[:], y_hi[:].bitcast(F32), ALU.subtract, tally=to_pe)
                for j in range(KT // 2):
                    for m2 in range(2):
                        pair = wait_product()
                        tt(z_a[:, m2], pair, rn[:], tally=free)
                        first()
                    for m2 in range(2):
                        wait_act()
                    for m2 in range(2):
                        m = 2 * j + m2
                        pair = wait_product()
                        tt(z_d[:], pair, z_a[:, m2], tally=free)
                        pair = wait_product()
                        cp(z_b[:], pair, tally=free)
                        first()
                        wait_act()
                        tt(z_d[:], z_d[:], z_c[:])
                        tt(merged[:, KT - 1 - m], merged[:, KT - 1 - m], z_d[:], ALU.add)
                first()
                for m in range(KT):
                    wait_act()
                    tt(ua_lo[:, m], merged[:, m], ua_hi[:, m].bitcast(F32), ALU.subtract, tally=to_pe)
                dve.wait_ge(s_hload, 16 * KT)
                for m in range(KT):
                    residual(m, 1.0)
                    first()
                    boundary(m, *after_mix, 2)
            if do_att:
                def evac_q(m):
                    def go(pair):
                        tt(sq[:], pair, rn[:], tally=free)
                        first()
                        wait_act()
                        tt(ua_lo[:, m], sq[:], ua_hi[:, m].bitcast(F32), ALU.subtract,
                           tally=to_pe if m == KT - 1 else step)
                    return go
                evacuate_after_norm(evac_q(0))
                for m in range(1, KT):
                    evac_q(m)(wait_product())

                probs = Tally(s_prob)

                def softmax(j):
                    pair = wait_product()
                    assert (prod.n - 1) % 4 == score_pair[j]
                    link(v.tensor_reduce(stat[:, 0], pair.rearrange("p (t n) -> p t n", t=4), AX, ALU.max))
                    ts(stat[:, 1], stat[:, 0], -(HD ** -0.5), None, tally=to_act)
                    wait_act()
                    first(free)
                    link(v.reciprocal(stat[:, 0], stat[:, 2]))
                    tt(prob[:, j % 2], prob[:, j % 2], stat[:, 0].unsqueeze(2).to_broadcast([P, 4, N_MEM]), tally=probs)

                def split(hi, lo, src):
                    cp(hi, src)
                    tt(lo, src, hi.bitcast(F32), ALU.subtract, tally=free)

                softmax(0)
                softmax(1)
                for j in range(2 * HEADS):
                    pair = wait_product().rearrange("p (c n) -> p c n", c=2)
                    split(pt_hi[:], pt_lo[:], pair)
                    first(to_pe)
                    if j + 2 < 2 * HEADS:
                        softmax(j + 2)
                    pair = wait_product().rearrange("p (c n) -> p c n", c=2)
                    hd, c = j // 2, j % 2
                    cols = slice(c * HALF, (c + 1) * HALF)
                    split(ub_hi[:, 2 * hd:2 * hd + 2, cols], ub_lo[:, 2 * hd:2 * hd + 2, cols], pair)
                    if c == 1:
                        first()
                first(to_pe)
                dve.wait_ge(s_hload, 16 * KT * (2 if do_mix else 1))
                for m in range(KT):
                    residual(m, 1.0)
                    first()
                    boundary(m, *after_att, 4)
            if do_f2:
                ffn(None, None, 0)
            root_factor(L)
            for m in range(KT):
                stt(h[:, m], h[:, m], gains[:, 5, m:m + 1], rn[:], ALU.mult, ALU.mult, tally=to_act)


def stages_units(stages):
    out = []
    if "A" in stages:
        out += [("k", m) for m in range(KT)] + [("v", k) for k in range(KT)]
    def ffn(f):
        gu = lambda j: [(f"{f}_w_gate", j), (f"{f}_w_up", j)]
        seq = gu(0) + gu(1)
        for i in range(1, FT // 2):
            seq += gu(2 * i) + gu(2 * i + 1) + [(f"{f}_down", 2 * i - 2), (f"{f}_down", 2 * i - 1)]
        return seq + [(f"{f}_down", FT - 2), (f"{f}_down", FT - 1)]
    if "1" in stages:
        out += ffn("ffn1")
    if "M" in stages:
        out += [("w_in", 4), ("w_in", 5)] + [("w_in", m) for m in range(4)]
        out += [("w_in", 6 + m) for m in range(KT)]
        out += [("pool_proj", j) for j in range(KT // 2)]
        for j in range(KT // 2):
            out += [("w_in", 14 + 2 * j), ("w_in", 15 + 2 * j), ("glu", j)]
        out += [("mix_out", m) for m in range(KT)]
    if "A" in stages:
        out += [("w_q", m) for m in range(KT)] + [("w_xo", m) for m in range(KT)]
    if "2" in stages:
        out += ffn("ffn2")
    return out


def pack(inputs, stages):
    w = {k: np.asarray(x)[0] for k, x in inputs.items() if k.startswith(("w_", "ffn")) and np.asarray(x).ndim == 3}

    def cols(x, m, width=P):
        kt = x.shape[0] // P
        return x[:, m * P:(m + 1) * P].reshape(kt, P, P).transpose(1, 0, 2).reshape(P, kt * P)

    out = np.empty((len(stages_units(stages)), P, D), np.float32)
    for u, (n, m) in enumerate(stages_units(stages)):
        if n == "k":
            t = cols(w["w_kv"], m)
        elif n == "v":
            t = w["w_kv"][m * P:(m + 1) * P, D:]
        elif n.endswith("_down"):
            t = w[n[:4] + "_w_down"][m * P:(m + 1) * P]
        elif n == "pool_proj":
            t = np.concatenate([cols(w["w_pool_proj"], 2 * m + q) for q in range(2)], 1)
        elif n == "glu":
            t = np.concatenate([cols(w[x], 2 * m + q) for q in range(2) for x in ("w_glu_val", "w_glu_gate")], 1)
        elif n == "mix_out":
            t = cols(w["w_mix_out"], m).reshape(P, KT, P)[:, ::-1].reshape(P, D)
        else:
            t = cols(w[n], m)
        out[u] = t
    return out


STAGES = "1MA2"


def kernel(**inputs):
    from concourse import bacc
    from concourse.bass_utils import run_bass_kernel_spmd

    f = {k: np.asarray(x) for k, x in inputs.items()}
    A = np.ascontiguousarray
    arrays = {"weights": pack(inputs, STAGES)}
    arrays["x"] = A(f["x"][0].T.reshape(KT, P, L))
    arrays["mem"] = A(f["mem"][0].T.reshape(KT, P, N_MEM).transpose(1, 0, 2))
    norms = [f["ffn1_norm"][0], f["mix_norm"][0], f["xattn_norm"][0], f["mem_norm"][0], f["ffn2_norm"][0], f["final_norm"]]
    arrays["gains"] = A(np.stack(norms).reshape(6, KT, P).transpose(2, 0, 1))
    arrays["pool_scale"] = A(f["pool_scale"][0].reshape(4, P).T)
    arrays["pool_w"] = A(f["pool_w"][0].transpose(1, 0, 2))
    arrays["dskip"] = A(f["ssm_d"][0].reshape(G, HG).T)
    ar, ai = f["ssm_a_re"][0], f["ssm_a_im"][0]
    ld = np.broadcast_to(f["ssm_log_dt"][0][:, :, None], ar.shape)
    el = np.stack([x.reshape(2, G * S) for x in (ar, ai, ld)], 1)
    arrays["el_a"] = A(np.broadcast_to(el[:, :, None, :], (2, 3, P, G * S)))
    b = [f[k][0].transpose(0, 3, 1, 2).reshape(2, HG, G * S) for k in ("ssm_b_re", "ssm_b_im")]
    arrays["el_b"] = A(np.tile(np.stack(b, 1), (1, 1, T, 1)))
    pl = lambda x: x.reshape(2, PAIRS, P).transpose(2, 0, 1).reshape(P, COLS)
    arrays["pl_a"] = A(np.stack([pl(x) for x in (ar, ai, ld)]))
    bp = [f[k][0].reshape(2, PAIRS, P, HG) for k in ("ssm_b_re", "ssm_b_im")]
    cp = [f[k][0].transpose(0, 1, 3, 2).reshape(2, PAIRS, P, HG) for k in ("ssm_c_re", "ssm_c_im")]
    arrays["pl_bc"] = A(np.stack([x.transpose(2, 0, 1, 3).reshape(P, COLS * HG) for x in bp + cp], 1).reshape(P, -1))
    e = np.arange(T + 1, dtype=np.float32)
    ke = np.stack([e, T - e])[:, None, :]
    arrays["kexp"] = A(np.broadcast_to(np.broadcast_to(ke, (2, PAIRS, T + 1)).reshape(1, -1), (P, COLS * (T + 1))))
    arrays["nidx"] = A(np.broadcast_to(np.arange(NC, dtype=np.float32), (P, NC)))
    i = np.repeat(np.arange(T, dtype=np.float32), HG)
    arrays["kcol"] = A(np.stack([T - 1 - i, i], 1))
    arrays["ones"], arrays["ident"] = np.ones((P, P), np.float32), np.eye(P, dtype=np.float32)
    arrays["eye"] = np.eye(HG, dtype=np.float32)
    edge = np.empty((4, 2, PAD), np.float32)
    for g, w in enumerate(WINDOWS):
        for side, t in enumerate((np.arange(PAD), np.arange(L - PAD, L))):
            count = np.minimum(t + w - w // 2, L) - np.maximum(t - w // 2, 0)
            edge[g, side] = w / count
    arrays["edge"] = A(np.broadcast_to(edge, (P, 4, 2, PAD)))

    nc = bacc.Bacc("TRN2", target_bir_lowering=False, num_devices=1)
    aps = {n: nc.dram_tensor(f"in_{n}", x.shape, F32, kind="ExternalInput").ap() for n, x in arrays.items()}
    aps["out"] = nc.dram_tensor("out", (KT, P, L), F32, kind="ExternalOutput").ap()
    build(nc, aps, STAGES)
    r = run_bass_kernel_spmd(nc, [{f"in_{n}": x for n, x in arrays.items()}], core_ids=[0])
    return r.results[0]["out"].reshape(D, L).T.reshape(1, L, D)
```

```python
import numpy as np
import concourse.bass as bass
from concourse import mybir
from contextlib import ExitStack

F32 = mybir.dt.float32
F32R = mybir.dt.float32r
ALU = mybir.AluOpType
ACT = mybir.ActivationFunctionType
AX = mybir.AxisListType.X

P = 128
D = 1024
L = 1024
KT = D // P
HALF = 512
F_FF = 2816
FT = F_FF // P
N_MEM = 256
HEADS = 4
HD = D // HEADS
WINDOWS = (2, 4, 8, 16)
PAD = max(WINDOWS) // 2
G = 16
HG = 16
S = 64
T = P // HG
NC = L // T
PAIRS = G // 2
COLS = 2 * PAIRS
DIAGS = 2 * T - 1
EPS = 1e-6
RING = 3
RAW = 2
UNITS = 16 + 2 * 3 * FT + 2 + 4 + 16 + 4 + 4 + 8 + 8 + 8

INV_2PI = float(np.float32(1 / (2 * np.pi)))
ROUND = 1.5 * 2.0 ** 23
TWO_PI_HI = 6.28125
TWO_PI_LO = float(np.float32(2 * np.pi - 6.28125))
PI_IN = 3.1415925


class Tally:

    def __init__(self, sem):
        self.sem, self.n, self.i, self.stride, self.base = sem, 0, None, 0, 0

    def add(self, k=1):
        self.n += k
        return self.at()

    def at(self, back=0):
        v = self.n - back
        return v if self.i is None else v + self.i * self.stride

    def enter(self, i, stride):
        self.i, self.stride, self.base = i, stride, self.n

    def leave(self, trips, name=""):
        got = self.n - self.base
        assert got == self.stride, (self.sem, got, self.stride)
        self.n, self.i = self.base + got * trips, None


def build(nc, a, stages):
    ctx = ExitStack()
    with ctx:
        def sem(name):
            return ctx.enter_context(nc.semaphore(name))

        def tensors(where, specs):
            return [where.enter_context(nc.sbuf_tensor(n, s, d)) for n, s, d in specs]

        w_hi, w_lo, raw = tensors(ctx, [("w_hi", [P, RING, KT, P], F32R), ("w_lo", [P, RING, KT, P], F32R),
                                        ("raw", [P, RAW, D], F32)])
        rn, acc, sq = tensors(ctx, [("rn", [P, L], F32), ("acc", [P, L], F32), ("sq", [P, L], F32)])
        gains, ones, ident = tensors(ctx, [("gains", [P, 6, KT], F32), ("ones", [P, P], F32), ("ident", [P, P], F32)])
        pscale, m8, dskip, edge, eye = tensors(ctx, [
            ("pscale", [P, 4], F32), ("m8", [P, COLS], F32), ("dskip", [HG, G], F32),
            ("edge", [P, 4, 2, PAD], F32), ("eye", [HG, HG], F32)])
        stat, norm, tick = tensors(ctx, [("stat", [P, 4, 4], F32), ("norm", [P, 4, L // P], F32), ("tick", [P, 2], F32)])
        with ExitStack() as v:
            mem_t, mem_w, mn_hi, mn_lo, kv_hi, kv_lo = tensors(v, [
                ("mem_t", [P, KT, N_MEM], F32), ("mem_w", [P, KT, N_MEM], F32),
                ("mn_hi", [P, KT, N_MEM], F32R), ("mn_lo", [P, KT, N_MEM], F32R),
                ("kv_hi", [P, 2, KT * N_MEM], F32R), ("kv_lo", [P, 2, KT * N_MEM], F32R)])
        hidden_specs = (("act_hi", [P, 2, 2, L], F32R), ("act_lo", [P, 2, 2, L], F32R),
                        ("f_gate", [P, L], F32), ("f_silu", [P, L], F32), ("f_up", [P, L], F32), ("f_act", [P, L], F32))
        with ExitStack() as v:
            hidden_a = tensors(v, [(n + "_a", x, d) for n, x, d in hidden_specs])
        ua_hi, ua_lo = tensors(ctx, [("ua_hi", [P, KT, L], F32R), ("ua_lo", [P, KT, L], F32R)])
        with ExitStack() as v:
            prep = tensors(v, [("prep", [P, 2 * KT * L], F32)])[0]
        with ExitStack() as v:
            hidden_b = tensors(v, [(n + "_b", x, d) for n, x, d in hidden_specs])
        with ExitStack() as v:
            mx_lowest, mx_v, mx_a, mx_b = tensors(v, [
                ("mx_pooled", [P, 2, 2, L], F32R), ("mx_v", [P, L + 2 * PAD], F32),
                ("mx_a", [P, L + 2 * PAD], F32), ("mx_b", [P, L + 2 * PAD], F32)])
        pooled = mx_lowest
        with ExitStack() as v:
            merged, mixed_hi, mixed_lo = tensors(v, [
                ("merged", [P, KT, L], F32), ("mixed_hi", [P, 4, L], F32R), ("mixed_lo", [P, 4, L], F32R)])
        with ExitStack() as v:
            merged_again, z_a, z_b, z_c, z_d = tensors(v, [
                ("merged_again", [P, KT, L], F32), ("z_a", [P, 2, L], F32), ("z_b", [P, L], F32),
                ("z_c", [P, L], F32), ("z_d", [P, L], F32)])
        ub_hi, ub_lo = tensors(ctx, [("ub_hi", [P, KT, L], F32R), ("ub_lo", [P, KT, L], F32R)])
        step_specs = (("e_m", [P, 2, 2, P], F32), ("f_m", [P, 2, 2, P], F32), ("m_m", [P, 2, P], F32),
                      ("tab", [P, 2, 2, NC], F32))
        with ExitStack() as v:
            u_t = tensors(v, [("u_t", [P, G, NC], F32)])[0]
            with ExitStack() as w:
                s_perm, pw_raw, pw_hi, pw_lo = tensors(w, [
                    ("s_perm", [P, 2, T, NC], F32), ("pw_raw", [P, 4, P], F32),
                    ("pw_hi", [P, 4, P], F32R), ("pw_lo", [P, 4, P], F32R)])
            step_sets = [tensors(v, [(f"{n}{k}", x, d) for n, x, d in step_specs]) for k in range(2)]
            sw, st_, sx, y_t = tensors(v, [
                ("sw", [P, 2, 2, NC], F32), ("st_", [P, 2, 2, NC], F32),
                ("sx", [P, 2, 2, NC + 1], F32), ("y_t", [P, 2, 2, NC], F32)])
        with ExitStack() as v:
            y_in, y_g, y_hi, y_lo = tensors(v, [
                ("y_in", [P, 2, T, NC], F32), ("y_g", [P, 2, L], F32),
                ("y_hi", [P, 2, L], F32R), ("y_lo", [P, 2, L], F32R)])
        with ExitStack() as v:
            k_hi, k_lo, v_hi, v_lo, pt_hi, pt_lo, prob = tensors(v, [
                ("k_hi", [P, 2, 2, N_MEM], F32R), ("k_lo", [P, 2, 2, N_MEM], F32R),
                ("v_hi", [P, 2, 2, HD], F32R), ("v_lo", [P, 2, 2, HD], F32R),
                ("pt_hi", [P, 2, HALF], F32R), ("pt_lo", [P, 2, HALF], F32R),
                ("prob", [P, 2, 4, N_MEM], F32)])
        h = tensors(ctx, [("h", [P, KT, L], F32)])[0]
        ps = [ctx.enter_context(nc.psum_tensor(f"ps{i}", [P, 2, HALF], F32)) for i in range(4)]

        def scratch(name, shape, dt=F32):
            return nc.dram_tensor(name, shape, dt).ap()

        d_kv_hi, d_kv_lo = (scratch(n, (2, P, KT * N_MEM)) for n in ("d_kv_hi", "d_kv_lo"))
        d_e, d_f = scratch("d_e", (P, 2, 2, G * S)), scratch("d_f", (P, 2, COLS, (T + 1) * HG))
        d_tab, d_k = scratch("d_tab", (P, 2, COLS, NC)), scratch("d_k", (HG, G, DIAGS * HG))
        d_m, d_s, d_y = scratch("d_m", (P, G, P)), scratch("d_s", (T, G * HG, NC)), scratch("d_y", (P, G, NC))
        d_h = scratch("d_h", (KT, P, L))

        raw_landed = [sem(f"raw_landed{i}") for i in range(RAW)]
        s_w_hi, s_w_split, s_w_used = sem("w_hi_written"), sem("w_split"), sem("w_used")
        s_prod, s_free = sem("product_done"), sem("psum_pair_free")
        s_dve = sem("dve_step")
        s_d2a, s_a2d, s_d2p = sem("dve_for_act"), sem("act_for_dve"), sem("dve_for_pe")
        s_const, s_mem, s_pl = (sem(n) for n in ("const_loaded", "mem_loaded", "pl_loaded"))
        s_x, s_q, s_norm = sem("x_loaded"), sem("q_split"), sem("squares_summed")
        s_estore, s_pstore, s_kstore, s_mstore, s_kvstore = (sem(n) for n in
            ("e_stored", "tab_f_stored", "k_stored", "m_stored", "kv_stored"))
        s_hspill, s_hload, s_pw, s_sst, s_uld = (sem(n) for n in
            ("h_spilled", "h_reloaded", "pool_w_loaded", "s_stored", "u_loaded"))
        s_step = [sem("ssm_step_loaded0"), sem("ssm_step_loaded1")]
        s_yst, s_yld = [sem("y_stored0"), sem("y_stored1")], sem("y_loaded")
        s_kvld = [sem("kv_loaded0"), sem("kv_loaded1")]
        s_out, s_tick = sem("out_stored"), sem("tick_written")
        s_prob = sem("probabilities_normalised")
        block = ctx.enter_context(nc.Block())

        do_f1, do_mix, do_att, do_f2 = (c in stages for c in "1MA2")
        after_att = (ub_hi, ub_lo) if do_f2 else (None, None)
        after_mix = (ub_hi, ub_lo) if do_att or do_f2 else (None, None)
        after_f1 = (ua_hi, ua_lo) if do_mix else after_mix
        u_hi, u_lo = (ub_hi, ub_lo) if stages[0] in "A2" else (ua_hi, ua_lo)
        score_pair, turn_pair, att_pair, glu_pair = {}, {}, {}, {}
        units = len(stages_units(stages))
        def pc(k, w=D):
            return prep[:, k:k + w]

        PL = {n: pc(k * COLS, COLS) for k, n in enumerate(
            ("ar", "ai", "ld", "dtar", "rr", "s", "c", "t1", "t2", "t3", "t4", "qr", "qi", "mag", "r8"))}
        o = 512
        p_b = prep[:, o:o + 4 * 256].rearrange("p (q c x) -> p q c x", q=4, c=COLS)
        o += 1024
        p_bb = prep[:, o:o + 2 * 256].rearrange("p (q c x) -> p q c x", q=2, c=COLS)
        o += 512
        NE = COLS * (T + 1)
        kexp, k_ang, k_mag, k_s, k_c, k_t = (pc(o + q * NE, NE) for q in range(6))
        o += 6 * NE
        nidx = pc(o, NC)
        o += NC
        NCA = NE * HG
        low, mid = o, o + 2 * NCA
        NT, NEE = COLS * NC, 2 * COLS * P
        ee = prep[:, low:low + NEE].rearrange("p (q c e x) -> p q c e x", q=2, c=COLS, e=T)
        kp = prep[0:HG, low:low + G * DIAGS * HG].rearrange("p (g d x) -> p g d x", g=G, d=DIAGS)
        ca = prep[:, mid:mid + 2 * NCA].rearrange("p (q c e x) -> p q c e x", q=2, c=COLS, e=T + 1)
        t_r, t_s, t_c = (pc(mid + q * NT, NT) for q in range(3))
        tmp_at = mid + 2 * NCA
        ca_t = prep[:, tmp_at:tmp_at + NCA].rearrange("p (c e x) -> p c e x", c=COLS, e=T + 1)
        assert NEE <= 2 * NCA and G * DIAGS * HG <= 2 * NCA and tmp_at + NCA <= 2 * KT * L
        e_out = [pc(mid + 2 * NCA + dr * 2 * D, 2 * D) for dr in range(2)]
        assert mid + 2 * NCA + 4 * D <= 2 * KT * L

        @block.sync
        def _(sp):
            def load(u, slot):
                sp.dma_start(raw[:, slot, :], a["weights"][u]).then_inc(raw_landed[slot], 16)

            for u in range(RAW):
                load(u, u)
            with sp.Fori(0, (units - RAW) // RAW) as i:
                for j in range(RAW):
                    sp.wait_ge(s_w_split, i * RAW + j + 1)
                    load(i * RAW + (RAW + j), j)

        @block.gpsimd
        def _(pool):
            def split(u, k, slot, wait_used=True):
                pool.wait_ge(raw_landed[k % RAW], 16 * (k // RAW + 1) if u is None else (u * (16 // RAW) + 16 * (k // RAW + 1)))
                if wait_used:
                    pool.wait_ge(s_w_used, k - RING + 1 if u is None else u + (k - RING + 1))
                if u is not None:
                    nc.gpsimd.tensor_tensor(tick[:, 1:2], tick[:, 0:1], tick[:, 0:1], op=ALU.add)
                hi, lo = w_hi[:, slot].rearrange("p k c -> p (k c)"), w_lo[:, slot].rearrange("p k c -> p (k c)")
                nc.gpsimd.tensor_scalar(hi, raw[:, k % RAW, :], 1.0, 0.0, ALU.mult, ALU.add).then_inc(s_w_hi, 1)
                pool.wait_ge(s_w_hi, k + 1 if u is None else u + (k + 1))
                nc.gpsimd.tensor_tensor(lo, raw[:, k % RAW, :], hi.bitcast(F32), op=ALU.subtract).then_inc(s_w_split, 1)

            body = RING * RAW
            nc.gpsimd.memset(tick[:], 0.0).then_inc(s_tick, 1)
            pool.wait_ge(s_tick, 1)
            for k in range(body):
                split(None, k, k % RING, k >= RING)
            trips = (units - body) // body
            with pool.Fori(0, trips) as i:
                for j in range(body):
                    split(i * body, body + j, j % RING)
            for k in range(body * (trips + 1), units):
                split(None, k, k % RING)

        @block.tensor
        def _(pe):
            unit, used, prod = Tally(s_w_split), Tally(s_w_used), Tally(s_prod)
            free, ready = Tally(s_free), Tally(s_d2p)
            all_tallies = (unit, used, prod, free, ready)
            owed = [0]

            def mm(out, lhsT, rhs, start, stop, done=False):
                ins = nc.tensor.matmul(out, lhsT, rhs, start=start, stop=stop)
                if done:
                    prod.add()
                    ins.then_inc(s_prod, 1)
                elif owed[0]:
                    owed[0] -= 1
                    used.add()
                    ins.then_inc(s_w_used, 1)
                return ins

            def take_unit():
                pe.wait_ge(s_w_split, unit.add())
                return (unit.n - 1) % RING

            def take_pair():
                k = prod.n + taken[0]
                if k >= 4:
                    pe.wait_ge(s_free, prod.at(4 - 1 - taken[0]))
                return ps[k % 4]
            taken = [0]

            def wait_dve():
                pe.wait_ge(s_d2p, ready.add())

            def three(out, whi, wlo, xhi, xlo, first, last, cols, done=False):
                for c, (o_c, x_c) in enumerate(cols):
                    mm(o_c(out), whi, x_c(xhi), first, False)
                    mm(o_c(out), whi, x_c(xlo), False, False)
                for c, (o_c, x_c) in enumerate(cols):
                    mm(o_c(out), wlo, x_c(xhi), False, last, done and c == len(cols) - 1)

            HALVES = [(lambda t, c=c: t[:, c, :], lambda x, c=c: x[:, c * HALF:(c + 1) * HALF]) for c in range(2)]

            def product(whi, wlo, xhi, xlo, tiles, t0=0, each=None, order=None):
                pair = take_pair()
                order = order or range(tiles)
                for k in order:
                    if each:
                        each()
                    three(pair, whi[:, t0 + k], wlo[:, t0 + k], xhi[:, k], xlo[:, k], k == order[0], k == order[-1],
                          HALVES, done=(k == order[-1]))

            def unit_product(xhi, xlo, each=None, order=None):
                s = take_unit()
                product(w_hi[:, s], w_lo[:, s], xhi, xlo, KT, each=each, order=order)
                owed[0] += 1

            def opening(xhi, xlo):
                unit_product(xhi, xlo, each=wait_dve)
                unit_product(xhi, xlo)
                tile = iter(range(KT))
                unit_product(xhi, xlo, each=lambda: sum_squares(L, ahead=1) if next(tile) == KT // 2 else None)
                spread(L)

            def sum_squares(width, ahead=0):
                taken[0] = ahead
                pair = take_pair()
                taken[0] = 0
                wait_dve()
                for c in range(width // P):
                    ins = nc.tensor.matmul(pair[:, 0, c:c + 1], acc[:, c * P:(c + 1) * P], ones[:, 0:1], start=True, stop=True)
                ins.then_inc(s_norm, 1)

            def spread(width):
                pair = take_pair()
                wait_dve()
                n = max(1, width // HALF)
                w = width // n
                for c in range(n):
                    mm(pair[:, c, 0:w], ones[:], sq[:, c * w:(c + 1) * w], True, True, done=(c == n - 1))

            if do_att:
                sum_squares(N_MEM)
                spread(N_MEM)
                one = [(lambda t: t[:, 0, 0:N_MEM], lambda x: x)]
                for m in range(KT):
                    s = take_unit()
                    pair = take_pair()
                    for k in range(KT):
                        if m == 0:
                            wait_dve()
                        three(pair, w_hi[:, s, k], w_lo[:, s, k], mn_hi[:, k], mn_lo[:, k], k == 0, k == KT - 1,
                              one, done=(k == KT - 1))
                    owed[0] += 1
                pairs = []
                for t in range(2):
                    taken[0] = t
                    pairs.append(take_pair())
                taken[0] = 0
                for k in range(KT):
                    s = take_unit()
                    wh, wl = (w[:, s].rearrange("p k c -> p (k c)") for w in (w_hi, w_lo))
                    for t in range(2):
                        rows = slice(t * P, (t + 1) * P)
                        for c in range(2):
                            cs = slice(c * HALF, (c + 1) * HALF)
                            mm(pairs[t][:, c], mn_hi[:, k, rows], wh[:, cs], k == 0, False)
                            mm(pairs[t][:, c], mn_hi[:, k, rows], wl[:, cs], False, False)
                        for c in range(2):
                            cs = slice(c * HALF, (c + 1) * HALF)
                            mm(pairs[t][:, c], mn_lo[:, k, rows], wh[:, cs], False, k == KT - 1,
                               done=(k == KT - 1 and c == 1))
                    owed[0] += 1
            if do_mix:
                wait_dve()
                for dr in range(2):
                    for ri in range(2):
                        pair = take_pair()
                        for j in range(PAIRS):
                            ins = nc.tensor.transpose(pair[:, j // 4, (j % 4) * P:(j % 4 + 1) * P],
                                                      ee[:, ri, dr * PAIRS + j].rearrange("p e x -> p (e x)"), ident[:])
                        prod.add()
                        ins.then_inc(s_prod, 1)
                wait_dve()
                for dr in range(2):
                    for gh in range(2):
                        pair = take_pair()
                        for g8 in range(8):
                            g = gh * 8 + g8
                            rows = slice((g % 2) * S, (g % 2 + 1) * S)
                            col = dr * PAIRS + g // 2
                            for q in range(2):
                                mm(pair[0:HG, g8 % 2, (g8 // 2) * P:(g8 // 2 + 1) * P], p_bb[rows, q, col, :],
                                   ca[rows, q, col, dr:dr + T, :].rearrange("p e x -> p (e x)"), q == 0, q == 1,
                                   done=(q == 1 and g8 == 7))

            def ffn(xhi, xlo, mem):
                act_hi, act_lo = mem[:2]

                def down(b, act_ready=True):
                    sl = [take_unit(), take_unit()]
                    for m in range(KT):
                        pair = take_pair()
                        for k in range(2):
                            if m == 0:
                                wait_dve()
                            if m == KT - 1 and k == 1:
                                owed[0] += 1
                            three(pair, w_hi[:, sl[k], m], w_lo[:, sl[k], m], act_hi[:, b, k], act_lo[:, b, k],
                                  k == 0, k == 1, HALVES, done=(k == 1))
                    owed[0] += 1

                opening(xhi, xlo)
                unit_product(xhi, xlo)
                with pe.Fori(0, FT // 4) as i:
                    for t, stride in zip(all_tallies, (12, 12, 24, 0, 4)):
                        t.enter(i, stride)
                    for b in range(2):
                        for _ in range(4):
                            unit_product(xhi, xlo)
                        down(b)
                    for t in all_tallies:
                        t.leave(FT // 4)
                down(0)

            if do_f1:
                ffn(ua_hi, ua_lo, hidden_b)
            if do_mix:
                opening(ua_hi, ua_lo)
                unit_product(ua_hi, ua_lo)

                def pool_mix(g):
                    pair = take_pair()
                    wait_dve()
                    three(pair, pw_hi[:, g], pw_lo[:, g], pooled[:, g % 2, 0], pooled[:, g % 2, 1], True, True,
                          HALVES, done=True)

                def ssm_states(q):
                    pair = take_pair()
                    e_m = step_sets[q % 2][0]
                    wait_dve()
                    for ri in range(2):
                        for dr in range(2):
                            for gg in range(2):
                                rhs = u_t[:, 2 * q + gg, :] if dr == 0 else u_t[:, 2 * q + gg, ::-1]
                                mm(pair[gg * S:(gg + 1) * S, ri, dr * NC:(dr + 1) * NC], e_m[:, dr, ri, gg * S:(gg + 1) * S],
                                   rhs, True, True, done=(ri == 1 and dr == 1 and gg == 1))

                def ssm_out(q):
                    pair = take_pair()
                    _, f_m, m_m, _ = step_sets[q % 2]
                    wait_dve()
                    for gg in range(2):
                        rows = slice(gg * S, (gg + 1) * S)
                        out = pair[:, gg, 0:NC]
                        mm(out, m_m[:, gg, :], u_t[:, 2 * q + gg, :], True, False)
                        for dr in range(2):
                            for ri in range(2):
                                x = sx[rows, ri, dr, 0:NC] if dr == 0 else sx[rows, ri, dr, 0:NC][:, ::-1]
                                mm(out, f_m[rows, ri, dr, :], x, False, dr == 1 and ri == 1,
                                   done=(dr == 1 and ri == 1 and gg == 1))

                pool_mix(0)
                unit_product(ua_hi, ua_lo)
                pool_mix(1)
                unit_product(ua_hi, ua_lo)
                unit_product(ua_hi, ua_lo)
                pool_mix(2)
                pool_mix(3)

                def pool_proj():
                    s = take_unit()
                    for m2 in range(2):
                        product(w_hi[:, s], w_lo[:, s], mixed_hi, mixed_lo, 4, t0=4 * m2)
                    owed[0] += 1

                for q in range(PAIRS):
                    ssm_states(q)
                    if q + 1 < PAIRS:
                        unit_product(ua_hi, ua_lo)
                    else:
                        pool_proj()
                    ssm_out(q)
                for j in range(1, KT // 2):
                    pool_proj()
                wait_dve()
                for j in range(KT // 2):
                    s = take_unit()
                    for m2 in range(2):
                        glu_pair[2 * j + m2] = prod.n % 4
                        for gv in range(2):
                            product(w_hi[:, s], w_lo[:, s], y_hi, y_lo, 2, t0=4 * m2 + 2 * gv)
                    owed[0] += 1
                    unit_product(ua_hi, ua_lo)
                    unit_product(ua_hi, ua_lo)
                for m in range(KT):
                    unit_product(ua_hi, ua_lo, each=wait_dve if m == 0 else None, order=range(KT - 1, -1, -1))
            if do_att:
                def scores(j):
                    hd, c = j // 2, j % 2
                    score_pair[j] = prod.n % 4
                    pair = take_pair()
                    if c == 0:
                        pe.wait_ge(s_q, 2 * (hd + 1))
                        pe.wait_ge(s_kvld[hd % 2], 64 * (hd // 2 + 1))
                    for t in range(4):
                        cols = slice(c * HALF + t * P, c * HALF + (t + 1) * P)
                        out = pair[:, t // 2, (t % 2) * N_MEM:(t % 2 + 1) * N_MEM]
                        for d in range(2):
                            qh, ql = ua_hi[:, 2 * hd + d, cols], ua_lo[:, 2 * hd + d, cols]
                            mm(out, qh, k_hi[:, hd % 2, d], d == 0, False)
                            mm(out, qh, k_lo[:, hd % 2, d], False, False)
                            mm(out, ql, k_hi[:, hd % 2, d], False, d == 1, done=(d == 1 and t == 3))

                def turn(j):
                    turn_pair[j] = prod.n % 4
                    pair = take_pair()
                    pe.wait_ge(s_prob, j + 1)
                    for t in range(4):
                        for mt in range(2):
                            ins = nc.tensor.transpose(pair[:, mt, t * P:(t + 1) * P],
                                                      prob[:, j % 2, t, mt * P:(mt + 1) * P], ident[:])
                    prod.add()
                    ins.then_inc(s_prod, 1)

                def attend(j):
                    hd = j // 2
                    att_pair[j] = prod.n % 4
                    pair = take_pair()
                    wait_dve()
                    for d in range(2):
                        for mt in range(2):
                            vh, vl = (x[:, hd % 2, mt, d * P:(d + 1) * P] for x in (v_hi, v_lo))
                            mm(pair[:, d], vh, pt_hi[:, mt], mt == 0, False)
                            mm(pair[:, d], vh, pt_lo[:, mt], False, False)
                            mm(pair[:, d], vl, pt_hi[:, mt], False, mt == 1, done=(mt == 1 and d == 1))

                opening(ub_hi, ub_lo)
                unit_product(ub_hi, ub_lo)
                scores(0)
                unit_product(ub_hi, ub_lo)
                scores(1)
                for j in range(2 * HEADS):
                    turn(j)
                    if j + 2 < 2 * HEADS:
                        scores(j + 2)
                    attend(j)
                    if j < 3:
                        unit_product(ub_hi, ub_lo)
                wait_dve()
                for m in range(KT):
                    unit_product(ua_hi, ua_lo)
            if do_f2:
                ffn(ub_hi, ub_lo, hidden_a)
            sum_squares(L)
            spread(L)
            assert unit.n == units, (unit.n, units)

        @block.scalar
        def _(act):
            from_dve, to_dve = Tally(s_d2a), Tally(s_a2d)
            kv_loads = [0, 0]

            def wait_dve():
                act.wait_ge(s_d2a, from_dve.add())

            def run(out, in_, func, last=True, **kw):
                ins = nc.scalar.activation(out, in_, func, **kw)
                if last:
                    to_dve.add()
                    ins.then_inc(s_a2d, 1)
                return ins

            def one(out, in_, func, **kw):
                wait_dve()
                run(out, in_, func, **kw)

            def load(dst, src, s):
                act.dma_start(dst, src).then_inc(s, 16)

            load(mem_t[:], a["mem"], s_mem)
            for dst, n in ((gains, "gains"), (ones, "ones"), (ident, "ident"), (pscale, "pool_scale"), (dskip, "dskip"),
                           (edge, "edge"), (eye, "eye")):
                load(dst[:], a[n], s_const)
            if do_mix:
                for k, n in enumerate(("ar", "ai", "ld")):
                    load(PL[n], a["pl_a"][k], s_pl)
                load(prep[:, 512:1536], a["pl_bc"], s_pl)
                load(kexp, a["kexp"], s_pl)
                load(nidx, a["nidx"], s_pl)
            for k in range(KT):
                load(h[:, k], a["x"][k], s_x)

            def root(n=L // P):
                one(norm[:, 1, 0:n], norm[:, 0, 0:n], ACT.Sqrt)

            def trig(r, s, c):
                wait_dve()
                run(s, r, ACT.Sin, last=False)
                run(c, r, ACT.Sin, scale=0.5)

            if do_att:
                root(N_MEM // P)
            if do_mix:
                one(PL["t1"], PL["ld"], ACT.Exp)
                one(PL["mag"], PL["dtar"], ACT.Exp)
                trig(PL["rr"], PL["s"], PL["c"])
                wait_dve()
                run(m8[:], PL["dtar"], ACT.Exp, scale=float(T))
                one(k_mag, k_mag, ACT.Exp)
                trig(k_ang, k_s, k_c)

            def store_half(n):
                if do_att:
                    wait_dve()
                    for d, t in ((d_kv_hi, kv_hi), (d_kv_lo, kv_lo)):
                        load(d[n], t[:, n].bitcast(F32), s_kvstore)

            store_half(0)
            if do_mix:
                wait_dve()
                load(d_f, ca[:].rearrange("p q c e x -> p q c (e x)"), s_pstore)
            store_half(1)
            if do_mix:
                for dr in range(2):
                    wait_dve()
                    load(d_e[:, dr].rearrange("p r c -> p (r c)"), e_out[dr], s_estore)

            def store_kernels():
                if do_mix:
                    wait_dve()
                    load(d_k, kp[:].rearrange("p g d x -> p g (d x)"), s_kstore)

            def split_high(m, dst, gi):
                if dst is not None:
                    one(dst[:, m], h[:, m], ACT.Copy, scale=gains[:, gi, m:m + 1])

            def squares(last, between):
                for m in range(KT):
                    if last or m > 2:
                        wait_dve()
                    run(acc[:] if m == 0 else (rn, sq)[m % 2][:], h[:, m], ACT.Square)
                    if m == 2 and between:
                        between()

            def boundary(dst, gi, between=None):
                for m in range(KT):
                    split_high(m, dst, gi)
                squares(dst is None, between)

            def ffn(next_dst, gi, mem, after_root=lambda: None):
                act_hi, _, f_gate, f_silu, _, f_act = mem
                root()
                after_root()

                def hidden(b, t):
                    one(f_silu[:], f_gate[:], ACT.Silu)
                    one(act_hi[:, b, t], f_act[:], ACT.Copy)
                for t in range(2):
                    hidden(0, t)
                with act.Fori(0, FT // 4) as i:
                    from_dve.enter(i, 8)
                    to_dve.enter(i, 8)
                    for b in range(2):
                        for t in range(2):
                            hidden(1 - b, t)
                    from_dve.leave(FT // 4)
                    to_dve.leave(FT // 4)
                boundary(next_dst, gi)

            boundary(u_hi, 0, store_kernels)
            if do_mix:
                trig(t_r, t_s, t_c)
                wait_dve()
                for k, t in enumerate((t_c, t_s)):
                    load(d_tab[:, k].rearrange("p c n -> p (c n)"), t, s_pstore)

            def store_m():
                if do_mix:
                    act.wait_ge(s_kstore, 16)
                    for i in range(T):
                        load(d_m[HG * i:HG * (i + 1)], d_k[:, :, (T - 1 - i) * HG:(T - 1 - i) * HG + P], s_mstore)

            if do_f1:
                ffn(after_f1[0], 1, hidden_b, store_m)
            if do_mix:
                for m in range(KT):
                    load(d_h[m], h[:, m], s_hspill)
                root()
                if not do_f1:
                    store_m()
                act.wait_ge(s_hspill, 16 * KT)
                load(pw_raw[:], a["pool_w"], s_pw)
                for t in range(2):
                    wait_dve()
                    load(d_s[:, t * P:(t + 1) * P, :].rearrange("i c n -> c i n"), s_perm[:, t], s_sst)
                    if t == 1:
                        act.wait_ge(s_sst, 32)
                        for i in range(T):
                            load(u_t[HG * i:HG * (i + 1)], d_s[i].rearrange("(g c) n -> c g n", c=HG), s_uld)
                act.wait_ge(s_estore, 32)
                act.wait_ge(s_pstore, 48)
                act.wait_ge(s_mstore, 16 * T)

                def load_step(q):
                    e_m, f_m, m_m, tab = step_sets[q % 2]
                    arrived = s_step[q % 2]
                    load(e_m[:], d_e[:, :, :, q * P:(q + 1) * P], arrived)
                    load(m_m[:], d_m[:, 2 * q:2 * q + 2, :], arrived)
                    for dr in range(2):
                        load(f_m[:, :, dr], d_f[:, :, dr * PAIRS + q, (1 - dr) * HG:(1 - dr) * HG + P], arrived)
                        load(tab[:, :, dr], d_tab[:, :, dr * PAIRS + q, :], arrived)

                load_step(0)

                def gate(m):
                    one(merged[:, KT - 1 - m], merged[:, KT - 1 - m], ACT.Sigmoid)

                gate(0)
                wait_dve()
                load_step(1)
                for q in range(PAIRS):
                    if q + 1 < PAIRS:
                        gate(q + 1)
                    wait_dve()
                    load(d_y[:, 2 * q:2 * q + 2, :], y_t[:, q % 2], s_yst[q % 2])
                    if q + 2 < PAIRS:
                        load_step(q + 2)
                for k in range(2):
                    act.wait_ge(s_yst[k], 16 * PAIRS // 2)
                for g in range(G):
                    load(y_in[HG * (g % 8):HG * (g % 8 + 1), g // 8],
                         d_y[:, g, :].rearrange("(i c) n -> c i n", c=HG), s_yld)
                act.wait_ge(s_yld, 16 * G)
                for t in range(2):
                    run(y_g[:, t].rearrange("p (n i) -> p i n", i=T), y_in[:, t], ACT.Gelu_apprx_tanh, last=(t == 1))
                def high(m):
                    run(ua_hi[:, KT - 1 - m], merged[:, KT - 1 - m], ACT.Copy)

                for m in range(KT):
                    if m % 2 == 0:
                        for m2 in range(2):
                            wait_dve()
                            run(z_b[:], ps[glu_pair[m + m2]][:].rearrange("p c n -> p (c n)"), ACT.Sigmoid)
                    if m == KT - 1:
                        wait_dve()
                        high(0)
                        high(1)
                    one(z_d[:], z_c[:], ACT.Sigmoid)
                for m in range(2, KT - 1):
                    high(m)
                wait_dve()
                high(KT - 1)
                for m in range(KT):
                    load(h[:, m], d_h[m], s_hload)
                boundary(after_mix[0], 2 if do_att else 4)
            if do_att:
                for m in range(KT):
                    load(d_h[m], h[:, m], s_hspill)
                root()
                act.wait_ge(s_hspill, 16 * KT * (2 if do_mix else 1))
                act.wait_ge(s_kvstore, 64)

                def load_kv(hd):
                    for src, kd, vd in ((d_kv_hi, k_hi, v_hi), (d_kv_lo, k_lo, v_lo)):
                        load(kd[:, hd % 2].bitcast(F32), src[0].rearrange("p (m t) -> p m t", m=KT)[:, 2 * hd:2 * hd + 2], s_kvld[hd % 2])
                        load(vd[:, hd % 2].bitcast(F32), src[1].rearrange("p (m d) -> p m d", m=2)[:, :, hd * HD:(hd + 1) * HD],
                             s_kvld[hd % 2])
                load_kv(0)
                load_kv(1)

                def split_q(m):
                    one(ua_hi[:, m], sq[:], ACT.Copy)

                def softmax(j):
                    wait_dve()
                    for t in range(4):
                        run(prob[:, j % 2, t], ps[score_pair[j]][:, t // 2, (t % 2) * N_MEM:(t % 2 + 1) * N_MEM], ACT.Exp,
                            last=(t == 3), bias=stat[:, 1, t:t + 1], scale=HD ** -0.5, accum_out=stat[:, 2, t:t + 1])
                for m in range(4):
                    split_q(m)
                softmax(0)
                split_q(4)
                softmax(1)
                for j in range(2 * HEADS):
                    one(pt_hi[:], ps[turn_pair[j]][:], ACT.Copy)
                    if j + 2 < 2 * HEADS:
                        softmax(j + 2)
                    hd, cols = j // 2, slice(j % 2 * HALF, (j % 2 + 1) * HALF)
                    one(ua_hi[:, 2 * hd:2 * hd + 2, cols], ps[att_pair[j]][:], ACT.Copy)
                    if j < 3:
                        split_q(5 + j)
                    if j % 2 == 1:
                        wait_dve()
                        if hd + 2 < HEADS:
                            load_kv(hd + 2)
                for m in range(KT):
                    load(h[:, m], d_h[m], s_hload)
                boundary(after_att[0], 4)
            if do_f2:
                ffn(None, 0, hidden_a)
            root()
            for m in range(KT):
                wait_dve()
                load(a["out"][m], h[:, m], s_out)
            act.wait_ge(s_out, 16 * KT)

        @block.vector
        def _(dve):
            step, prod, free = Tally(s_dve), Tally(s_prod), Tally(s_free)
            to_act, from_act, to_pe = Tally(s_d2a), Tally(s_a2d), Tally(s_d2p)
            norms = Tally(s_norm)
            all_tallies = (step, prod, free, to_act, from_act, to_pe)
            v = nc.vector

            def link(ins, tally=step):
                tally.add()
                ins.then_inc(tally.sem, 1)
                dve.wait_ge(tally.sem, tally.at())

            def wait_act():
                dve.wait_ge(s_a2d, from_act.add())

            def pair_of():
                return ps[(prod.n - 1) % 4]

            held = []

            def wait_product():
                if held:
                    if held[0] is not None:
                        return held.pop(0)
                    held.pop(0)
                    first(free)
                dve.wait_ge(s_prod, prod.add())
                return pair_of()[:].rearrange("p c n -> p (c n)")

            def tt(out, x, y, op=ALU.mult, tally=step):
                link(v.tensor_tensor(out, x, y, op), tally)

            def ts(out, x, s1, s2=None, op0=ALU.mult, op1=None, tally=step):
                if op1 is None:
                    link(v.tensor_scalar(out, x, s1, None, op0), tally)
                else:
                    link(v.tensor_scalar(out, x, s1, s2, op0, op1), tally)

            def stt(out, x, s, y, op0, op1, tally=step):
                link(v.scalar_tensor_tensor(out=out, in0=x, scalar=s, in1=y, op0=op0, op1=op1), tally)

            def cp(out, x, tally=step):
                link(v.tensor_copy(out, x), tally)

            def rounded(r, ang, k):
                ts(k, ang, INV_2PI, ROUND, ALU.mult, ALU.add)
                ts(k, k, ROUND, None, ALU.subtract)
                stt(r, k, -TWO_PI_HI, ang, ALU.mult, ALU.add)
                stt(r, k, -TWO_PI_LO, r, ALU.mult, ALU.add)
                ts(r, r, PI_IN, -PI_IN, ALU.min, ALU.max, tally=to_act)

            def cosine(c):
                wait_act()
                tt(c, c, c)
                ts(c, c, -2.0, 1.0, ALU.mult, ALU.add)

            def root_factor(w, keep=True):
                n = w // P
                dve.wait_ge(s_norm, norms.add())
                pair = ps[(prod.n % 4)]
                x, root, y, z = (norm[:, k, 0:n] for k in range(4))
                ts(x, pair[:, 0, 0:n], 1.0 / D, EPS, ALU.mult, ALU.add, tally=to_act)
                wait_act()
                link(v.reciprocal(y, root))
                tt(z, y, y)
                tt(z, z, x)
                ts(z, z, -0.5, 1.5, ALU.mult, ALU.add)
                tt(y, y, z)
                tt(sq[:, 0:w].rearrange("p (c t) -> p c t", c=n), ident[:].unsqueeze(1).to_broadcast([P, n, P]),
                   y.unsqueeze(2).to_broadcast([P, n, P]), tally=to_pe)
                pair = wait_product()[:, 0:w]
                if keep:
                    cp(rn[:, 0:w], pair)
                return pair

            def discretise(q, rows=None):
                wait_act()
                tt(q["dtar"], q["t1"], q["ar"], tally=to_act)
                tt(q["t2"], q["t1"], q["ai"])
                wait_act()
                rounded(q["rr"], q["t2"], q["t3"])
                tt(q["t1"], q["ar"], q["ar"])
                tt(q["t2"], q["ai"], q["ai"])
                tt(q["t1"], q["t1"], q["t2"], ALU.add)
                link(v.reciprocal(q["t4"], q["t1"]))
                cosine(q["c"])
                tt(q["t1"], q["mag"], q["c"])
                ts(q["t1"], q["t1"], 1.0, None, ALU.subtract)
                tt(q["t2"], q["mag"], q["s"])
                tt(q["qr"], q["t1"], q["ar"])
                tt(q["t3"], q["t2"], q["ai"])
                tt(q["qr"], q["qr"], q["t3"], ALU.add)
                tt(q["qr"], q["qr"], q["t4"])
                tt(q["qi"], q["t2"], q["ar"])
                tt(q["t3"], q["t1"], q["ai"])
                tt(q["qi"], q["qi"], q["t3"], ALU.subtract)
                tt(q["qi"], q["qi"], q["t4"])

            def complex_mult(re, im, ar, ai, br, bi, tmp, neg_im=False, tally=step, beside=lambda: None):
                tt(re, ar, br)
                tt(tmp, ai, bi)
                tt(re, re, tmp, ALU.subtract)
                beside()
                tt(im, ar, bi)
                tt(tmp, ai, br)
                if neg_im:
                    stt(im, im, -1.0, tmp, ALU.mult, ALU.subtract, tally=tally)
                else:
                    tt(im, im, tmp, ALU.add, tally=tally)

            def first(tally=to_act):
                link(v.memset(stat[:, 3, 0:1], 0.0), tally)

            dve.wait_ge(s_const, 16 * 7)
            if do_att:
                dve.wait_ge(s_mem, 16)
                tt(mem_w[:], mem_t[:], mem_t[:])
                link(v.tensor_reduce(acc[:, 0:N_MEM], mem_w[:].rearrange("p k t -> p t k"), AX, ALU.add), to_pe)
                root_factor(N_MEM)
                first(free)
                for k in range(KT):
                    stt(mem_w[:, k], mem_t[:, k], gains[:, 3, k:k + 1], rn[:, 0:N_MEM], ALU.mult, ALU.mult)
                    cp(mn_hi[:, k], mem_w[:, k])
                    tt(mn_lo[:, k], mem_w[:, k], mn_hi[:, k].bitcast(F32), ALU.subtract, tally=to_pe)
            kv_left = list(range(KT + 2)) if do_att else []

            def store_kv():
                if not kv_left:
                    return
                m = kv_left.pop(0)
                pair = wait_product()
                if m < KT:
                    hi, lo, src = kv_hi[:, 0, m * N_MEM:(m + 1) * N_MEM], kv_lo[:, 0, m * N_MEM:(m + 1) * N_MEM], pair[:, 0:N_MEM]
                else:
                    n = m - KT
                    hi, lo, src = kv_hi[:, 1, n * D:(n + 1) * D], kv_lo[:, 1, n * D:(n + 1) * D], pair
                cp(hi, src)
                tt(lo, src, hi.bitcast(F32), ALU.subtract, tally=free)
                if m in (KT - 1, KT + 1):
                    first()

            if do_mix:
                q = PL
                dve.wait_ge(s_pl, 96)
                first()
                discretise(q)
                store_kv()
                store_kv()
                bro = lambda t: t.unsqueeze(2).to_broadcast([P, COLS, HG])
                complex_mult(p_bb[:, 0], p_bb[:, 1], bro(q["qr"]), bro(q["qi"]), p_b[:, 0], p_b[:, 1],
                             prep[:, tmp_at:tmp_at + COLS * HG].rearrange("p (c x) -> p c x", c=COLS))
                ts(q["t4"], q["rr"], float(T), None)
                turn8 = q["r8"]
                ts(q["t3"], q["t4"], INV_2PI, ROUND, ALU.mult, ALU.add)
                ts(q["t3"], q["t3"], ROUND, None, ALU.subtract)
                stt(turn8, q["t3"], -TWO_PI_HI, q["t4"], ALU.mult, ALU.add)
                stt(turn8, q["t3"], -TWO_PI_LO, turn8, ALU.mult, ALU.add, tally=to_act)
                wait_act()
                store_kv()
                e3 = lambda t: t.rearrange("p (c e) -> p c e", c=COLS)
                be = lambda t: t.unsqueeze(2).to_broadcast([P, COLS, T + 1])
                tt(e3(k_mag), e3(kexp), be(q["dtar"]), tally=to_act)
                tt(e3(k_t), e3(kexp), be(q["rr"]))
                wait_act()
                rounded(k_ang, k_t, k_c)
                store_kv()
                cosine(k_c)
                tt(k_s, k_s, k_mag)
                tt(k_c, k_c, k_mag)
                for dr in range(2):
                    cols = slice(dr * PAIRS, (dr + 1) * PAIRS)
                    shape = [P, PAIRS, T, HG]
                    pw = [(e3(k)[:, cols, T - 1::-1] if dr == 0 else e3(k)[:, cols, T:0:-1]).unsqueeze(3).to_broadcast(shape)
                          for k in (k_c, k_s)]
                    bb = [p_bb[:, x, cols].unsqueeze(2).to_broadcast(shape) for x in range(2)]
                    work = prep[:, tmp_at:tmp_at + PAIRS * P].rearrange("p (c e x) -> p c e x", c=PAIRS, e=T)
                    complex_mult(ee[:, 0, cols], ee[:, 1, cols], *pw, *bb, work, tally=to_pe if dr else step,
                                 beside=store_kv)
                    store_kv()
                w4 = lambda t: e3(t).unsqueeze(3).to_broadcast([P, COLS, T + 1, HG])
                c4 = lambda k: p_b[:, k].unsqueeze(2).to_broadcast([P, COLS, T + 1, HG])
                complex_mult(ca[:, 0], ca[:, 1], w4(k_c), w4(k_s), c4(2), c4(3), ca_t, neg_im=True, tally=to_act)
                first(to_pe)
            while kv_left:
                store_kv()
            if do_mix:
                for dr in range(2):
                    for ri in range(2):
                        pair = wait_product()
                        cp(e_out[dr][:, ri * D:(ri + 1) * D], pair, tally=free)
                    first()

            def kernels_out(k):
                dr, gh = k // 2, k % 2
                wait_product()
                pair = pair_of()[0:HG].rearrange("p c (g e x) -> p c g e x", g=4, e=T)
                for c in range(2):
                    out, src = kp[:, gh * 8 + c:gh * 8 + 8:2], pair[:, c]
                    end = free if c else step
                    if dr == 0:
                        cp(out[:, :, T - 1:DIAGS], src, tally=end)
                    else:
                        cp(out[:, :, 0:T - 1], src[:, :, 0:T - 1])
                        tt(out[:, :, T - 1], out[:, :, T - 1], src[:, :, T - 1], ALU.add, tally=end)

            def skip_connection():
                for g in range(G):
                    stt(kp[:, g, T - 1], eye[:], dskip[:, g:g + 1], kp[:, g, T - 1], ALU.mult, ALU.add,
                        tally=to_act if g == G - 1 else step)

            def boundary(dst_hi, dst_lo, gi, new=None, between=None):
                def low(m):
                    wait_act()
                    stt(dst_lo[:, m], h[:, m], gains[:, gi, m:m + 1], dst_hi[:, m].bitcast(F32),
                        ALU.mult, ALU.subtract, tally=to_pe)

                def add(m):
                    wait_act()
                    if m:
                        tt(acc[:], acc[:], (rn, sq)[m % 2][:], ALU.add,
                           tally=to_pe if m == KT - 1 else to_act if dst_hi is not None and m + 2 < KT else step)

                for m in range(KT):
                    if new:
                        new(m)
                    first()
                    if m:
                        (low if dst_hi is not None else add)(m - 1)
                if dst_hi is None:
                    add(KT - 1)
                else:
                    low(KT - 1)
                    if between:
                        between()
                    for m in range(KT):
                        add(m)

            def beside_x(m):
                if m == 1 and do_att:
                    dve.wait_ge(s_kvstore, 64)
                if m >= 2 and m % 2 == 0 and do_mix:
                    kernels_out(m // 2 - 1)

            def last_kernels():
                kernels_out(3)
                skip_connection()

            dve.wait_ge(s_x, 16 * KT)
            boundary(u_hi, u_lo, 0, beside_x, last_kernels if do_mix else None)
            if do_mix:
                dve.wait_ge(s_pstore, 16)
                dve.wait_ge(s_estore, 32)
                r3 = lambda t: t.rearrange("p (c n) -> p c n", c=COLS)
                tt(r3(t_c), turn8.unsqueeze(2).to_broadcast([P, COLS, NC]), nidx.unsqueeze(1).to_broadcast([P, COLS, NC]))
                rounded(t_r, t_c, t_s)
                cosine(t_c)
                first()

            def residual(m, coef):
                pair = wait_product()
                link(v.scalar_tensor_tensor(out=h[:, m], in0=pair, scalar=coef, in1=h[:, m], op0=ALU.mult, op1=ALU.add), free)

            def opening():
                prod.add(3)
                held.extend([ps[(prod.n - 3 + k) % 4][:].rearrange("p c n -> p (c n)") for k in range(3)])
                pairs = list(held)
                held.clear()
                root_factor(L)
                held.extend(pairs + [None])
                if do_mix:
                    dve.wait_ge(s_pstore, 48)
                    dve.wait_ge(s_kstore, 16)

            def ffn(next_hi, next_lo, gi, mem):
                act_hi, act_lo, f_gate, f_silu, f_up, f_act = mem

                def hidden(b, t):
                    pair = wait_product()
                    tt(f_gate[:], pair, rn[:], tally=free)
                    first()
                    pair = wait_product()
                    tt(f_up[:], pair, rn[:], tally=free)
                    wait_act()
                    tt(f_act[:], f_silu[:], f_up[:], tally=to_act)
                    wait_act()
                    tt(act_lo[:, b, t], f_act[:], act_hi[:, b, t].bitcast(F32), ALU.subtract, tally=to_pe)

                opening()
                hidden(0, 0)
                hidden(0, 1)
                with dve.Fori(0, FT // 4) as i:
                    for t, stride in zip(all_tallies, (0, 24, 24, 8, 8, 4)):
                        t.enter(i, stride)
                    for b in range(2):
                        for t in range(2):
                            hidden(1 - b, t)
                        for m in range(KT):
                            residual(m, 0.5)
                    for t in all_tallies:
                        t.leave(FT // 4)
                boundary(next_hi, next_lo, gi, lambda m: residual(m, 0.5))

            if do_f1:
                ffn(*after_f1, 1, hidden_b)
            if do_mix:
                opening()
                dve.wait_ge(s_hspill, 16 * KT)
                for t in range(2):
                    pair = wait_product()
                    tt(s_perm[:, t].rearrange("p i n -> p n i"), pair.rearrange("p (n i) -> p n i", i=T),
                       rn[:].rearrange("p (n i) -> p n i", i=T), tally=free)
                    first()
                dve.wait_ge(s_pw, 16)
                cp(pw_hi[:], pw_raw[:])
                tt(pw_lo[:], pw_raw[:], pw_hi[:].bitcast(F32), ALU.subtract)
                for t in (mx_v, mx_a, mx_b):
                    link(v.memset(t[:], 0.0))

                def pool(g):
                    pair = wait_product()
                    w = WINDOWS[g]
                    tt(mx_v[:, PAD:PAD + L], pair, rn[:], tally=free)
                    n = L + 2 * PAD
                    tt(mx_a[:, 1:n], mx_v[:, 0:n - 1], mx_v[:, 1:n], ALU.add)
                    cur, nxt, size = mx_a, mx_b, 2
                    while size < w:
                        k = size // 2
                        tt(nxt[:, k:n - k], cur[:, 0:n - 2 * k], cur[:, 2 * k:n], ALU.add)
                        cur, nxt, size = nxt, cur, 2 * size
                    for side in range(2):
                        cols = slice(PAD, 2 * PAD) if side == 0 else slice(L, L + PAD)
                        tt(cur[:, cols], cur[:, cols], edge[:, g, side])
                    stt(nxt[:, PAD:PAD + L], cur[:, PAD:PAD + L], 1.0 / w, mx_v[:, PAD:PAD + L], ALU.mult, ALU.subtract)
                    hi, lo = pooled[:, g % 2, 0], pooled[:, g % 2, 1]
                    cp(hi, nxt[:, PAD:PAD + L])
                    tt(lo, nxt[:, PAD:PAD + L], hi.bitcast(F32), ALU.subtract, tally=to_pe)

                def pool_mixed(g):
                    pair = wait_product()
                    ts(mx_v2[:], pair, pscale[:, g:g + 1], tally=free)
                    cp(mixed_hi[:, g], mx_v2[:])
                    tt(mixed_lo[:, g], mx_v2[:], mixed_hi[:, g].bitcast(F32), ALU.subtract)
                mx_v2 = acc

                pool(0)
                pool(1)
                pool_mixed(0)
                pool(2)
                pool_mixed(1)
                pool(3)

                def gate(m):
                    tt(merged[:, KT - 1 - m], wait_product(), rn[:], tally=free)
                    first()

                def project(m):
                    tt(merged[:, KT - 1 - m], merged[:, KT - 1 - m], wait_product(), tally=free)

                gate(0)
                pool_mixed(2)
                pool_mixed(3)
                first()
                wait_act()
                link(v.memset(sx[:], 0.0))
                dve.wait_ge(s_uld, 16 * T)
                for q in range(PAIRS):
                    dve.wait_ge(s_step[q % 2], 96 * (q // 2 + 1))
                    tab = step_sets[q % 2][3]
                    first(to_pe)
                    pair = wait_product()
                    re, im = (pair[:, k * HALF:k * HALF + 2 * NC].rearrange("p (d n) -> p d n", d=2) for k in range(2))
                    ct, sn = tab[:, 0], tab[:, 1]
                    tt(sw[:, 0], re, ct)
                    tt(st_[:, 0], im, sn)
                    tt(sw[:, 0], sw[:, 0], st_[:, 0], ALU.add)
                    tt(sw[:, 1], im, ct)
                    tt(st_[:, 0], re, sn, tally=free)
                    tt(sw[:, 1], sw[:, 1], st_[:, 0], ALU.subtract)
                    for dr in range(2):
                        mag = m8[:, dr * PAIRS + q:dr * PAIRS + q + 1].to_broadcast([P, NC])
                        for ri in range(2):
                            link(v.tensor_tensor_scan(st_[:, ri, dr], mag, sw[:, ri, dr], 0.0, ALU.mult, ALU.add))
                    tt(sw[:, 0], st_[:, 0], ct)
                    tt(sw[:, 1], st_[:, 1], sn)
                    tt(sx[:, 0, :, 1:], sw[:, 0], sw[:, 1], ALU.subtract)
                    tt(sw[:, 0], st_[:, 1], ct)
                    tt(sw[:, 1], st_[:, 0], sn)
                    tt(sx[:, 1, :, 1:], sw[:, 0], sw[:, 1], ALU.add, tally=to_pe)
                    if q + 1 < PAIRS:
                        gate(q + 1)
                    else:
                        project(0)
                        project(1)
                    pair = wait_product()
                    if q >= 2:
                        dve.wait_ge(s_yst[q % 2], 16 * (q // 2))
                    cp(y_t[:, q % 2], pair.rearrange("p (g n) -> p g n", g=2)[:, :, 0:NC], tally=free)
                    first()
                    if q + 1 < PAIRS:
                        wait_act()
                for m in range(2, KT):
                    project(m)
                wait_act()
                cp(y_hi[:], y_g[:])
                tt(y_lo[:], y_g[:], y_hi[:].bitcast(F32), ALU.subtract, tally=to_pe)

                def merged_low(m):
                    wait_act()
                    at = KT - 1 - m
                    tt(ua_lo[:, at], merged[:, at], ua_hi[:, at].bitcast(F32), ALU.subtract, tally=to_pe)

                for m in range(KT):
                    if m % 2 == 0:
                        for m2 in range(2):
                            wait_product()
                            first()
                            wait_act()
                            first(free)
                            tt(z_a[:, m2], wait_product(), z_b[:], tally=free)
                    pair = wait_product()
                    if m == KT - 1:
                        first()
                    tt(z_c[:], pair, rn[:], tally=free)
                    first()
                    if m == KT - 1:
                        merged_low(0)
                        merged_low(1)
                    wait_act()
                    tt(z_d[:], z_d[:], z_a[:, m % 2])
                    tt(merged[:, KT - 1 - m], merged[:, KT - 1 - m], z_d[:], ALU.add)
                first()
                for m in range(2, KT):
                    merged_low(m)
                dve.wait_ge(s_hload, 16 * KT)
                boundary(*after_mix, 2 if do_att else 4, lambda m: residual(m, 1.0))
            if do_att:
                q_ready = Tally(s_q)

                def evac_q(m):
                    tt(sq[:], wait_product(), rn[:], tally=free)
                    first()
                    wait_act()
                    tt(ua_lo[:, m], sq[:], ua_hi[:, m].bitcast(F32), ALU.subtract, tally=q_ready)

                probs = Tally(s_prob)

                def scores_max(j):
                    pair = wait_product()
                    assert (prod.n - 1) % 4 == score_pair[j]
                    link(v.tensor_reduce(stat[:, 0], pair.rearrange("p (t n) -> p t n", t=4), AX, ALU.max))
                    ts(stat[:, 1], stat[:, 0], -(HD ** -0.5), None, tally=to_act)

                def normalise(j):
                    wait_act()
                    first(free)
                    link(v.reciprocal(stat[:, 0], stat[:, 2]))
                    tt(prob[:, j % 2], prob[:, j % 2], stat[:, 0].unsqueeze(2).to_broadcast([P, 4, N_MEM]), tally=probs)

                def low_half(lo, hi):
                    pair = wait_product()
                    first()
                    wait_act()
                    tt(lo, pair.rearrange("p (c n) -> p c n", c=2), hi.bitcast(F32), ALU.subtract, tally=free)

                opening()
                for m in range(4):
                    evac_q(m)
                scores_max(0)
                normalise(0)
                evac_q(4)
                scores_max(1)
                normalise(1)
                for j in range(2 * HEADS):
                    low_half(pt_lo[:], pt_hi[:])
                    first(to_pe)
                    if j + 2 < 2 * HEADS:
                        scores_max(j + 2)
                        normalise(j + 2)
                    hd, cols = j // 2, slice(j % 2 * HALF, (j % 2 + 1) * HALF)
                    low_half(ua_lo[:, 2 * hd:2 * hd + 2, cols], ua_hi[:, 2 * hd:2 * hd + 2, cols])
                    if j < 3:
                        evac_q(5 + j)
                    if j % 2 == 1:
                        first()
                first(to_pe)
                dve.wait_ge(s_hload, 16 * KT * (2 if do_mix else 1))
                boundary(*after_att, 4, lambda m: residual(m, 1.0))
            if do_f2:
                ffn(None, None, 0, hidden_a)
            factor = root_factor(L, keep=False)
            for m in range(KT):
                stt(h[:, m], h[:, m], gains[:, 5, m:m + 1], factor, ALU.mult, ALU.mult, tally=to_act)


def stages_units(stages):
    out = []
    if "A" in stages:
        out += [("k", m) for m in range(KT)] + [("v", k) for k in range(KT)]
    def ffn(f):
        gu = lambda j: [(f"{f}_w_gate", j), (f"{f}_w_up", j)]
        seq = gu(0) + gu(1)
        for i in range(1, FT // 2):
            seq += gu(2 * i) + gu(2 * i + 1) + [(f"{f}_down", 2 * i - 2), (f"{f}_down", 2 * i - 1)]
        return seq + [(f"{f}_down", FT - 2), (f"{f}_down", FT - 1)]
    if "1" in stages:
        out += ffn("ffn1")
    if "M" in stages:
        out += [("w_in", 4), ("w_in", 5)] + [("w_in", m) for m in range(4)]
        out += [("w_in", 6 + m) for m in range(KT)]
        out += [("pool_proj", j) for j in range(KT // 2)]
        for j in range(KT // 2):
            out += [("glu", j), ("w_in", 14 + 2 * j), ("w_in", 15 + 2 * j)]
        out += [("mix_out", m) for m in range(KT)]
    if "A" in stages:
        out += [("w_q", m) for m in range(KT)] + [("w_xo", m) for m in range(KT)]
    if "2" in stages:
        out += ffn("ffn2")
    return out


def pack(inputs, stages):
    w = {k: np.asarray(x)[0] for k, x in inputs.items() if k.startswith(("w_", "ffn")) and np.asarray(x).ndim == 3}

    def cols(x, m, width=P):
        kt = x.shape[0] // P
        return x[:, m * P:(m + 1) * P].reshape(kt, P, P).transpose(1, 0, 2).reshape(P, kt * P)

    out = np.empty((len(stages_units(stages)), P, D), np.float32)
    for u, (n, m) in enumerate(stages_units(stages)):
        if n == "k":
            t = cols(w["w_kv"], m)
        elif n == "v":
            t = w["w_kv"][m * P:(m + 1) * P, D:]
        elif n.endswith("_down"):
            t = w[n[:4] + "_w_down"][m * P:(m + 1) * P]
        elif n == "pool_proj":
            t = np.concatenate([cols(w["w_pool_proj"], 2 * m + q) for q in range(2)], 1)
        elif n == "glu":
            t = np.concatenate([cols(w[x], 2 * m + q) for q in range(2) for x in ("w_glu_gate", "w_glu_val")], 1)
        elif n == "mix_out":
            t = cols(w["w_mix_out"], m).reshape(P, KT, P)[:, ::-1].reshape(P, D)
        else:
            t = cols(w[n], m)
        out[u] = t
    return out


STAGES = "1MA2"


def kernel(**inputs):
    from concourse import bacc
    from concourse.bass_utils import run_bass_kernel_spmd

    f = {k: np.asarray(x) for k, x in inputs.items()}
    A = np.ascontiguousarray
    arrays = {"weights": pack(inputs, STAGES)}
    arrays["x"] = A(f["x"][0].T.reshape(KT, P, L))
    arrays["mem"] = A(f["mem"][0].T.reshape(KT, P, N_MEM).transpose(1, 0, 2))
    norms = [f["ffn1_norm"][0], f["mix_norm"][0], f["xattn_norm"][0], f["mem_norm"][0], f["ffn2_norm"][0], f["final_norm"]]
    arrays["gains"] = A(np.stack(norms).reshape(6, KT, P).transpose(2, 0, 1))
    arrays["pool_scale"] = A(f["pool_scale"][0].reshape(4, P).T)
    arrays["pool_w"] = A(f["pool_w"][0].transpose(1, 0, 2))
    arrays["dskip"] = A(f["ssm_d"][0].reshape(G, HG).T)
    ar, ai = f["ssm_a_re"][0], f["ssm_a_im"][0]
    ld = np.broadcast_to(f["ssm_log_dt"][0][:, :, None], ar.shape)
    pl = lambda x: x.reshape(2, PAIRS, P).transpose(2, 0, 1).reshape(P, COLS)
    arrays["pl_a"] = A(np.stack([pl(x) for x in (ar, ai, ld)]))
    bp = [f[k][0].reshape(2, PAIRS, P, HG) for k in ("ssm_b_re", "ssm_b_im")]
    cp = [f[k][0].transpose(0, 1, 3, 2).reshape(2, PAIRS, P, HG) for k in ("ssm_c_re", "ssm_c_im")]
    arrays["pl_bc"] = A(np.stack([x.transpose(2, 0, 1, 3).reshape(P, COLS * HG) for x in bp + cp], 1).reshape(P, -1))
    e = np.arange(T + 1, dtype=np.float32)
    ke = np.stack([e, T - e])[:, None, :]
    arrays["kexp"] = A(np.broadcast_to(np.broadcast_to(ke, (2, PAIRS, T + 1)).reshape(1, -1), (P, COLS * (T + 1))))
    arrays["nidx"] = A(np.broadcast_to(np.arange(NC, dtype=np.float32), (P, NC)))
    arrays["ones"], arrays["ident"] = np.ones((P, P), np.float32), np.eye(P, dtype=np.float32)
    arrays["eye"] = np.eye(HG, dtype=np.float32)
    edge = np.empty((4, 2, PAD), np.float32)
    for g, w in enumerate(WINDOWS):
        for side, t in enumerate((np.arange(PAD), np.arange(L - PAD, L))):
            count = np.minimum(t + w - w // 2, L) - np.maximum(t - w // 2, 0)
            edge[g, side] = w / count
    arrays["edge"] = A(np.broadcast_to(edge, (P, 4, 2, PAD)))

    nc = bacc.Bacc("TRN2", target_bir_lowering=False, num_devices=1)
    aps = {n: nc.dram_tensor(f"in_{n}", x.shape, F32, kind="ExternalInput").ap() for n, x in arrays.items()}
    aps["out"] = nc.dram_tensor("out", (KT, P, L), F32, kind="ExternalOutput").ap()
    build(nc, aps, STAGES)
    r = run_bass_kernel_spmd(nc, [{f"in_{n}": x for n, x in arrays.items()}], core_ids=[0])
    return r.results[0]["out"].reshape(D, L).T.reshape(1, L, D)
```

```python
import numpy as np
import concourse.bass as bass
from concourse import mybir
from contextlib import ExitStack

F32 = mybir.dt.float32
F32R = mybir.dt.float32r
ALU = mybir.AluOpType
ACT = mybir.ActivationFunctionType
AX = mybir.AxisListType.X

P = 128
D = 1024
L = 1024
KT = D // P
HALF = 512
F_FF = 2816
FT = F_FF // P
N_MEM = 256
HEADS = 4
HD = D // HEADS
WINDOWS = (2, 4, 8, 16)
PAD = max(WINDOWS) // 2
G = 16
HG = 16
S = 64
T = P // HG
NC = L // T
PAIRS = G // 2
COLS = 2 * PAIRS
DIAGS = 2 * T - 1
EPS = 1e-6
RING = 3
RAW = 2

INV_2PI = float(np.float32(1 / (2 * np.pi)))
ROUND = 1.5 * 2.0 ** 23
TWO_PI_HI = 6.28125
TWO_PI_LO = float(np.float32(2 * np.pi - 6.28125))
PI_IN = 3.1415925


class Tally:

    def __init__(self, sem):
        self.sem, self.n, self.i, self.stride, self.base = sem, 0, None, 0, 0

    def add(self, k=1):
        self.n += k
        return self.at()

    def at(self, back=0):
        v = self.n - back
        return v if self.i is None else v + self.i * self.stride

    def enter(self, i, stride):
        self.i, self.stride, self.base = i, stride, self.n

    def leave(self, trips):
        got = self.n - self.base
        assert got == self.stride, (self.sem, got, self.stride)
        self.n, self.i = self.base + got * trips, None


def build(nc, a, stages):
    ctx = ExitStack()
    with ctx:
        def sem(name):
            return ctx.enter_context(nc.semaphore(name))

        def tensors(where, specs):
            return [where.enter_context(nc.sbuf_tensor(n, s, d)) for n, s, d in specs]

        w_hi, w_lo, raw = tensors(ctx, [("w_hi", [P, RING, KT, P], F32R), ("w_lo", [P, RING, KT, P], F32R),
                                        ("raw", [P, RAW, D], F32)])
        acc = tensors(ctx, [("acc", [P, L], F32)])[0]
        with ExitStack() as v:
            diag_hi, diag_lo = tensors(v, [("diag_hi", [P, L], F32R), ("diag_lo", [P, L], F32R)])
        sq, rn = tensors(ctx, [("sq", [P, L], F32), ("rn", [P, L], F32)])
        gains, ones, ident = tensors(ctx, [("gains", [P, 6, KT], F32), ("ones", [P, P], F32), ("ident", [P, P], F32)])
        ones_r, norm_hi, nidx, turn8 = tensors(ctx, [("ones_r", [P, P], F32R), ("norm_hi", [P, L // P], F32R),
                                                     ("nidx", [P, NC], F32), ("turn8", [P, COLS], F32)])
        pscale, m8, dskip, edge, eye = tensors(ctx, [
            ("pscale", [P, 4], F32), ("m8", [P, COLS], F32), ("dskip", [2 * HG, PAIRS], F32),
            ("edge", [P, 4, 2, PAD], F32), ("eye", [2 * HG, HG], F32)])
        stat, norm, tick = tensors(ctx, [("stat", [P, 2, 4, 4], F32), ("norm", [P, 4, L // P], F32), ("tick", [P, 2], F32)])
        with ExitStack() as v:
            mem_t, mem_w, mn_hi, mn_lo, kv_hi, kv_lo = tensors(v, [
                ("mem_t", [P, KT, N_MEM], F32), ("mem_w", [P, KT, N_MEM], F32),
                ("mn_hi", [P, KT, N_MEM], F32R), ("mn_lo", [P, KT, N_MEM], F32R),
                ("kv_hi", [P, 2, KT * N_MEM], F32R), ("kv_lo", [P, 2, KT * N_MEM], F32R)])
        hidden_specs = (("act_hi", [P, 2, 2, L], F32R), ("act_lo", [P, 2, 2, L], F32R),
                        ("f_gate", [P, L], F32), ("f_silu", [P, L], F32), ("f_up", [P, L], F32), ("f_act", [P, L], F32))
        with ExitStack() as v:
            hidden_a = tensors(v, [(n + "_a", x, d) for n, x, d in hidden_specs])
        ua_hi, ua_lo = tensors(ctx, [("ua_hi", [P, KT, L], F32R), ("ua_lo", [P, KT, L], F32R)])
        with ExitStack() as v:
            prep = tensors(v, [("prep", [P, 2 * KT * L], F32)])[0]
        with ExitStack() as v:
            hidden_b = tensors(v, [(n + "_b", x, d) for n, x, d in hidden_specs])
        with ExitStack() as v:
            pooled, mx_v, mx_a, mx_b = tensors(v, [
                ("pooled", [P, 2, 2, L], F32R), ("mx_v", [P, L + 2 * PAD], F32),
                ("mx_a", [P, L + 2 * PAD], F32), ("mx_b", [P, L + 2 * PAD], F32)])
        with ExitStack() as v:
            merged, mixed_hi, mixed_lo = tensors(v, [
                ("merged", [P, KT, L], F32), ("mixed_hi", [P, 4, L], F32R), ("mixed_lo", [P, 4, L], F32R)])
        with ExitStack() as v:
            _, z_a, z_b, z_c, z_d = tensors(v, [
                ("merged_below", [P, KT, L], F32), ("z_a", [P, 2, L], F32), ("z_b", [P, 2, L], F32),
                ("z_c", [P, L], F32), ("z_d", [P, L], F32)])
        ub_hi, ub_lo = tensors(ctx, [("ub_hi", [P, KT, L], F32R), ("ub_lo", [P, KT, L], F32R)])
        step_specs = (("e_m", [P, 2, 2, P], F32), ("f_m", [P, 2, 2, P], F32), ("m_m", [P, 2, P], F32),
                      ("tab", [P, 2, 2, NC], F32))
        with ExitStack() as v:
            u_t = tensors(v, [("u_t", [P, G, NC], F32)])[0]
            with ExitStack() as w:
                s_perm, pw_raw, pw_hi, pw_lo = tensors(w, [
                    ("s_perm", [P, 2, T, NC], F32), ("pw_raw", [P, 4, P], F32),
                    ("pw_hi", [P, 4, P], F32R), ("pw_lo", [P, 4, P], F32R)])
            step_sets = [tensors(v, [(f"{n}{k}", x, d) for n, x, d in step_specs]) for k in range(2)]
            sw, st_, sx, y_t = tensors(v, [
                ("sw", [P, 2, 2, NC], F32), ("st_", [P, 2, 2, NC], F32),
                ("sx", [P, 2, 2, NC + 1], F32), ("y_t", [P, 2, 2, NC], F32)])
        with ExitStack() as v:
            y_in, y_g, y_hi, y_lo = tensors(v, [
                ("y_in", [P, 2, T, NC], F32), ("y_g", [P, 2, L], F32),
                ("y_hi", [P, 2, L], F32R), ("y_lo", [P, 2, L], F32R)])
        with ExitStack() as v:
            k_hi, k_lo, v_hi, v_lo, pt_hi, pt_lo, prob = tensors(v, [
                ("k_hi", [P, 2, 2, N_MEM], F32R), ("k_lo", [P, 2, 2, N_MEM], F32R),
                ("v_hi", [P, 2, 2, HD], F32R), ("v_lo", [P, 2, 2, HD], F32R),
                ("pt_hi", [P, 2, HALF], F32R), ("pt_lo", [P, 2, HALF], F32R),
                ("prob", [P, 2, 4, N_MEM], F32)])
        h = tensors(ctx, [("h", [P, KT, L], F32)])[0]
        ps = [ctx.enter_context(nc.psum_tensor(f"ps{i}", [P, 2, HALF], F32)) for i in range(4)]

        def scratch(name, shape, dt=F32):
            return nc.dram_tensor(name, shape, dt).ap()

        d_kv_hi, d_kv_lo = (scratch(n, (2, P, KT * N_MEM)) for n in ("d_kv_hi", "d_kv_lo"))
        d_e, d_f = scratch("d_e", (P, 2, 2, G * S)), scratch("d_f", (P, 2, COLS, (T + 1) * HG))
        d_tab, d_k = scratch("d_tab", (P, 2, COLS, NC)), scratch("d_k", (HG, G, DIAGS * HG))
        d_m, d_s, d_y = scratch("d_m", (P, G, P)), scratch("d_s", (T, G * HG, NC)), scratch("d_y", (P, G, NC))
        d_h = scratch("d_h", (KT, P, L))

        raw_landed = [sem(f"raw_landed{i}") for i in range(RAW)]
        s_w_hi, s_w_split, s_w_used = sem("w_hi_written"), sem("w_split"), sem("w_used")
        s_prod, s_free = sem("product_done"), sem("psum_pair_free")
        s_dve = sem("dve_step")
        s_d2a, s_a2d, s_d2p = sem("dve_for_act"), sem("act_for_dve"), sem("dve_for_pe")
        s_const, s_mem, s_pl = (sem(n) for n in ("const_loaded", "mem_loaded", "pl_loaded"))
        s_x, s_q, s_norm = sem("x_loaded"), sem("q_split"), sem("squares_summed")
        s_estore, s_pstore, s_kstore, s_mstore, s_kvstore = (sem(n) for n in
            ("e_stored", "tab_f_stored", "k_stored", "m_stored", "kv_stored"))
        s_hspill, s_hload, s_pw, s_sst, s_uld = (sem(n) for n in
            ("h_spilled", "h_reloaded", "pool_w_loaded", "s_stored", "u_loaded"))
        s_step = [sem("ssm_step_loaded0"), sem("ssm_step_loaded1")]
        s_yst, s_yld = [sem("y_stored0"), sem("y_stored1")], sem("y_loaded")
        s_k_in, s_v_in = [sem("k_loaded0"), sem("k_loaded1")], [sem("v_loaded0"), sem("v_loaded1")]
        s_out, s_tick = sem("out_stored"), sem("tick_written")
        s_prob = sem("probabilities_normalised")
        block = ctx.enter_context(nc.Block())

        do_f1, do_mix, do_att, do_f2 = (c in stages for c in "1MA2")
        after_att = (ub_hi, ub_lo) if do_f2 else (None, None)
        after_mix = (ub_hi, ub_lo) if do_att or do_f2 else (None, None)
        after_f1 = (ua_hi, ua_lo) if do_mix else after_mix
        u_hi, u_lo = (ub_hi, ub_lo) if stages[0] in "A2" else (ua_hi, ua_lo)
        finished = {}
        units = len(stages_units(stages))
        def pc(k, w=D):
            return prep[:, k:k + w]

        PL = {n: pc(k * COLS, COLS) for k, n in enumerate(
            ("ar", "ai", "ld", "dtar", "rr", "s", "c", "t1", "t2", "t3", "t4", "qr", "qi", "mag"))}
        o = 512
        p_b = prep[:, o:o + 4 * 256].rearrange("p (q c x) -> p q c x", q=4, c=COLS)
        o += 1024
        p_bb = prep[:, o:o + 2 * 256].rearrange("p (q c x) -> p q c x", q=2, c=COLS)
        o += 512
        NE = COLS * (T + 1)
        kexp, k_ang, k_mag, k_s, k_c, k_t = (pc(o + q * NE, NE) for q in range(6))
        o += 6 * NE
        NCA = NE * HG
        low, mid = o, o + 2 * NCA
        NT, NEE = PAIRS * NC, 2 * COLS * P
        ee = prep[:, low:low + NEE].rearrange("p (q c e x) -> p q c e x", q=2, c=COLS, e=T)
        kp = prep[0:2 * HG, low:low + PAIRS * DIAGS * HG].rearrange("p (g d x) -> p g d x", g=PAIRS, d=DIAGS)
        p_bd = [prep[:, at:at + COLS * 2 * HG].rearrange("p (c g x) -> p c g x", c=COLS, g=2) for at in (low + NEE, 512)]
        ca = prep[:, mid:mid + 2 * NCA].rearrange("p (q c e x) -> p q c e x", q=2, c=COLS, e=T + 1)
        tmp_at = tail = 12 * L
        ca_t = prep[:, tmp_at:tmp_at + NCA].rearrange("p (c e x) -> p c e x", c=COLS, e=T + 1)
        assert NEE + COLS * 2 * HG <= 2 * NCA and PAIRS * DIAGS * HG <= NEE and tmp_at + NCA <= 2 * KT * L
        e_out = [pc(tail + dr * 2 * D, 2 * D) for dr in range(2)]
        t_r, t_s, t_c = (pc(tail + q * NT, NT) for q in range(3))
        assert mid + 2 * NCA <= tail and tail + 4 * D <= 2 * KT * L

        def pt(j):
            if j == 2 * HEADS - 2:
                return [k[:].rearrange("p a b n -> p a (b n)") for k in (k_hi, k_lo)]
            return pt_hi[:], pt_lo[:]

        def kv_halves(m, pair):
            if m < KT:
                cols = slice(m * N_MEM, (m + 1) * N_MEM)
                return kv_hi[:, 0, cols], kv_lo[:, 0, cols], pair[:, 0:N_MEM]
            cols = slice((m - KT) * D, (m - KT + 1) * D)
            return kv_hi[:, 1, cols], kv_lo[:, 1, cols], pair

        @block.sync
        def _(sp):
            def load(u, slot):
                sp.dma_start(raw[:, slot, :], a["weights"][u]).then_inc(raw_landed[slot], 16)

            if do_att:
                sp.dma_start(mem_t[:], a["mem"]).then_inc(s_mem, 16)
            for u in range(RAW):
                load(u, u)
            with sp.Fori(0, (units - RAW) // RAW) as i:
                for j in range(RAW):
                    sp.wait_ge(s_w_split, i * RAW + j + 1)
                    load(i * RAW + (RAW + j), j)

        @block.gpsimd
        def _(pool):
            def split(u, k, slot, wait_used=True):
                pool.wait_ge(raw_landed[k % RAW], 16 * (k // RAW + 1) if u is None else (u * (16 // RAW) + 16 * (k // RAW + 1)))
                if wait_used:
                    pool.wait_ge(s_w_used, k - RING + 1 if u is None else u + (k - RING + 1))
                if u is not None:
                    nc.gpsimd.tensor_tensor(tick[:, 1:2], tick[:, 0:1], tick[:, 0:1], op=ALU.add)
                hi, lo = w_hi[:, slot].rearrange("p k c -> p (k c)"), w_lo[:, slot].rearrange("p k c -> p (k c)")
                nc.gpsimd.tensor_scalar(hi, raw[:, k % RAW, :], 1.0, 0.0, ALU.mult, ALU.add).then_inc(s_w_hi, 1)
                pool.wait_ge(s_w_hi, k + 1 if u is None else u + (k + 1))
                nc.gpsimd.tensor_tensor(lo, raw[:, k % RAW, :], hi.bitcast(F32), op=ALU.subtract).then_inc(s_w_split, 1)

            body = RING * RAW
            nc.gpsimd.memset(tick[:], 0.0).then_inc(s_tick, 1)
            pool.wait_ge(s_tick, 1)
            for k in range(body):
                split(None, k, k % RING, k >= RING)
            trips = (units - body) // body
            with pool.Fori(0, trips) as i:
                for j in range(body):
                    split(i * body, body + j, j % RING)
            for k in range(body * (trips + 1), units):
                split(None, k, k % RING)

        @block.tensor
        def _(pe):
            unit, used, prod = Tally(s_w_split), Tally(s_w_used), Tally(s_prod)
            free, ready = Tally(s_free), Tally(s_d2p)
            all_tallies = (unit, used, prod, free, ready)
            owed = [0]

            def mm(out, lhsT, rhs, start, stop, done=False):
                ins = nc.tensor.matmul(out, lhsT, rhs, start=start, stop=stop)
                if done:
                    prod.add()
                    ins.then_inc(s_prod, 1)
                elif owed[0]:
                    owed[0] -= 1
                    used.add()
                    ins.then_inc(s_w_used, 1)
                return ins

            def take_unit():
                pe.wait_ge(s_w_split, unit.add())
                return (unit.n - 1) % RING

            def take_pair():
                k = prod.n + taken[0]
                if k >= 4:
                    pe.wait_ge(s_free, prod.at(4 - 1 - taken[0]))
                return ps[k % 4]
            taken = [0]

            def wait_dve():
                pe.wait_ge(s_d2p, ready.add())

            def three(out, whi, wlo, xhi, xlo, first, last, cols, done=False):
                for c, (o_c, x_c) in enumerate(cols):
                    mm(o_c(out), whi, x_c(xhi), first, False)
                    mm(o_c(out), whi, x_c(xlo), False, False)
                for c, (o_c, x_c) in enumerate(cols):
                    mm(o_c(out), wlo, x_c(xhi), False, last, done and c == len(cols) - 1)

            HALVES = [(lambda t, c=c: t[:, c, :], lambda x, c=c: x[:, c * HALF:(c + 1) * HALF]) for c in range(2)]

            def product(whi, wlo, xhi, xlo, tiles, t0=0, each=None, order=None):
                pair = take_pair()
                order = order or range(tiles)
                for k in order:
                    if each:
                        each()
                    three(pair, whi[:, t0 + k], wlo[:, t0 + k], xhi[:, k], xlo[:, k], k == order[0], k == order[-1],
                          HALVES, done=(k == order[-1]))

            def unit_product(xhi, xlo, each=None, order=None):
                s = take_unit()
                product(w_hi[:, s], w_lo[:, s], xhi, xlo, KT, each=each, order=order)
                owed[0] += 1

            def opening(xhi, xlo):
                unit_product(xhi, xlo, each=wait_dve)
                unit_product(xhi, xlo)
                tile = iter(range(KT))
                unit_product(xhi, xlo, each=lambda: sum_squares(L, ahead=1) if next(tile) == KT // 2 else None)
                spread(L)

            def sum_squares(width, ahead=0):
                taken[0] = ahead
                pair = take_pair()
                taken[0] = 0
                wait_dve()
                for c in range(width // P):
                    ins = nc.tensor.matmul(pair[:, 0, c:c + 1], acc[:, c * P:(c + 1) * P], ones[:, 0:1], start=True, stop=True)
                ins.then_inc(s_norm, 1)

            def spread(width):
                pair = take_pair()
                wait_dve()
                n = max(1, width // HALF)
                w = width // n
                for c in range(n):
                    mm(pair[:, c, 0:w], ones_r[:], diag_hi[:, c * w:(c + 1) * w], True, False)
                    mm(pair[:, c, 0:w], ones_r[:], diag_lo[:, c * w:(c + 1) * w], False, True, done=(c == n - 1))

            if do_att:
                sum_squares(N_MEM)
                spread(N_MEM)
                one = [(lambda t: t[:, 0, 0:N_MEM], lambda x: x)]
                for m in range(KT):
                    s = take_unit()
                    pair = take_pair()
                    for k in range(KT):
                        if m == 0:
                            wait_dve()
                        three(pair, w_hi[:, s, k], w_lo[:, s, k], mn_hi[:, k], mn_lo[:, k], k == 0, k == KT - 1,
                              one, done=(k == KT - 1))
                    finished["kv", m] = prod.n
                    owed[0] += 1
                pairs = []
                for t in range(2):
                    taken[0] = t
                    pairs.append(take_pair())
                taken[0] = 0
                for k in range(KT):
                    s = take_unit()
                    wh, wl = (w[:, s].rearrange("p k c -> p (k c)") for w in (w_hi, w_lo))
                    for t in range(2):
                        rows = slice(t * P, (t + 1) * P)
                        for c in range(2):
                            cs = slice(c * HALF, (c + 1) * HALF)
                            mm(pairs[t][:, c], mn_hi[:, k, rows], wh[:, cs], k == 0, False)
                            mm(pairs[t][:, c], mn_hi[:, k, rows], wl[:, cs], False, False)
                        for c in range(2):
                            cs = slice(c * HALF, (c + 1) * HALF)
                            mm(pairs[t][:, c], mn_lo[:, k, rows], wh[:, cs], False, k == KT - 1,
                               done=(k == KT - 1 and c == 1))
                        if k == KT - 1:
                            finished["kv", KT + t] = prod.n
                    owed[0] += 1
            if do_mix:
                wait_dve()
                for dr in range(2):
                    for ri in range(2):
                        pair = take_pair()
                        for j in range(PAIRS):
                            ins = nc.tensor.transpose(pair[:, j // 4, (j % 4) * P:(j % 4 + 1) * P],
                                                      ee[:, ri, dr * PAIRS + j].rearrange("p e x -> p (e x)"), ident[:])
                        prod.add()
                        ins.then_inc(s_prod, 1)
                wait_dve()
                for dr in range(2):
                    pair = take_pair()
                    for p in range(PAIRS):
                        col = dr * PAIRS + p
                        for q in range(2):
                            mm(pair[0:2 * HG, p // 4, (p % 4) * P:(p % 4 + 1) * P], p_bd[q][:, col].rearrange("p g x -> p (g x)"),
                               ca[:, q, col, dr:dr + T, :].rearrange("p e x -> p (e x)"), q == 0, q == 1,
                               done=(q == 1 and p == PAIRS - 1))

            def ffn(xhi, xlo, mem):
                act_hi, act_lo = mem[:2]

                def down(b, act_ready=True):
                    sl = [take_unit(), take_unit()]
                    for m in range(KT):
                        pair = take_pair()
                        for k in range(2):
                            if m == 0:
                                wait_dve()
                            if m == KT - 1 and k == 1:
                                owed[0] += 1
                            three(pair, w_hi[:, sl[k], m], w_lo[:, sl[k], m], act_hi[:, b, k], act_lo[:, b, k],
                                  k == 0, k == 1, HALVES, done=(k == 1))
                    owed[0] += 1

                opening(xhi, xlo)
                unit_product(xhi, xlo)
                with pe.Fori(0, FT // 4) as i:
                    for t, stride in zip(all_tallies, (12, 12, 24, 0, 4)):
                        t.enter(i, stride)
                    for b in range(2):
                        for _ in range(4):
                            unit_product(xhi, xlo)
                        down(b)
                    for t in all_tallies:
                        t.leave(FT // 4)
                down(0)

            if do_f1:
                ffn(ua_hi, ua_lo, hidden_b)
            if do_mix:
                opening(ua_hi, ua_lo)
                unit_product(ua_hi, ua_lo)

                def pool_mix(g):
                    pair = take_pair()
                    wait_dve()
                    three(pair, pw_hi[:, g], pw_lo[:, g], pooled[:, g % 2, 0], pooled[:, g % 2, 1], True, True,
                          HALVES, done=True)

                def ssm_states(q):
                    pair = take_pair()
                    e_m = step_sets[q % 2][0]
                    wait_dve()
                    for ri in range(2):
                        for dr in range(2):
                            for gg in range(2):
                                rhs = u_t[:, 2 * q + gg, :] if dr == 0 else u_t[:, 2 * q + gg, ::-1]
                                mm(pair[gg * S:(gg + 1) * S, ri, dr * NC:(dr + 1) * NC], e_m[:, dr, ri, gg * S:(gg + 1) * S],
                                   rhs, True, True, done=(ri == 1 and dr == 1 and gg == 1))

                def ssm_out(q):
                    pair = take_pair()
                    _, f_m, m_m, _ = step_sets[q % 2]
                    wait_dve()
                    for gg in range(2):
                        rows = slice(gg * S, (gg + 1) * S)
                        out = pair[:, gg, 0:NC]
                        mm(out, m_m[:, gg, :], u_t[:, 2 * q + gg, :], True, False)
                        for dr in range(2):
                            for ri in range(2):
                                x = sx[rows, ri, dr, 0:NC] if dr == 0 else sx[rows, ri, dr, 0:NC][:, ::-1]
                                mm(out, f_m[rows, ri, dr, :], x, False, dr == 1 and ri == 1,
                                   done=(dr == 1 and ri == 1 and gg == 1))

                pool_mix(0)
                unit_product(ua_hi, ua_lo)
                pool_mix(1)
                unit_product(ua_hi, ua_lo)
                unit_product(ua_hi, ua_lo)
                pool_mix(2)
                pool_mix(3)

                def pool_proj():
                    s = take_unit()
                    for m2 in range(2):
                        product(w_hi[:, s], w_lo[:, s], mixed_hi, mixed_lo, 4, t0=4 * m2)
                    owed[0] += 1

                for q in range(PAIRS):
                    ssm_states(q)
                    if q + 1 < PAIRS:
                        unit_product(ua_hi, ua_lo)
                    else:
                        pool_proj()
                    ssm_out(q)
                for j in range(1, KT // 2):
                    pool_proj()
                wait_dve()
                for j in range(KT // 2):
                    s = take_unit()
                    for m2 in range(2):
                        for gv in range(2):
                            product(w_hi[:, s], w_lo[:, s], y_hi, y_lo, 2, t0=4 * m2 + 2 * gv)
                            if gv == 0:
                                finished["glu gate", 2 * j + m2] = prod.n
                    owed[0] += 1
                    unit_product(ua_hi, ua_lo)
                    unit_product(ua_hi, ua_lo)
                for m in range(KT):
                    unit_product(ua_hi, ua_lo, each=wait_dve if m == 0 else None, order=range(KT - 1, -1, -1))
            if do_att:
                def scores(j):
                    hd, c = j // 2, j % 2
                    pair = take_pair()
                    if c == 0:
                        pe.wait_ge(s_q, 2 * (hd + 1))
                        pe.wait_ge(s_k_in[hd % 2], 32 * (hd // 2 + 1))
                    for t in range(4):
                        cols = slice(c * HALF + t * P, c * HALF + (t + 1) * P)
                        out = pair[:, t // 2, (t % 2) * N_MEM:(t % 2 + 1) * N_MEM]
                        for d in range(2):
                            qh, ql = ua_hi[:, 2 * hd + d, cols], ua_lo[:, 2 * hd + d, cols]
                            mm(out, qh, k_hi[:, hd % 2, d], d == 0, False)
                            mm(out, qh, k_lo[:, hd % 2, d], False, False)
                            mm(out, ql, k_hi[:, hd % 2, d], False, d == 1, done=(d == 1 and t == 3))
                    finished["scores", j] = prod.n

                def turn(j):
                    pair = take_pair()
                    pe.wait_ge(s_prob, j + 1)
                    for t in range(4):
                        for mt in range(2):
                            ins = nc.tensor.transpose(pair[:, mt, t * P:(t + 1) * P],
                                                      prob[:, j % 2, t, mt * P:(mt + 1) * P], ident[:])
                    prod.add()
                    ins.then_inc(s_prod, 1)
                    finished["turn", j] = prod.n

                def attend(j):
                    hd = j // 2
                    pair = take_pair()
                    wait_dve()
                    if j % 2 == 0:
                        pe.wait_ge(s_v_in[hd % 2], 32 * (hd // 2 + 1))
                    p_hi, p_lo = pt(j)
                    for d in range(2):
                        for mt in range(2):
                            vh, vl = (x[:, hd % 2, mt, d * P:(d + 1) * P] for x in (v_hi, v_lo))
                            mm(pair[:, d], vh, p_hi[:, mt], mt == 0, False)
                            mm(pair[:, d], vh, p_lo[:, mt], False, False)
                            mm(pair[:, d], vl, p_hi[:, mt], False, mt == 1, done=(mt == 1 and d == 1))
                    finished["attend", j] = prod.n

                opening(ub_hi, ub_lo)
                unit_product(ub_hi, ub_lo)
                scores(0)
                unit_product(ub_hi, ub_lo)
                scores(1)
                for j in range(2 * HEADS):
                    if j + 2 < 2 * HEADS:
                        turn(j)
                        scores(j + 2)
                    if j < 3:
                        unit_product(ub_hi, ub_lo)
                    if 2 * HEADS - 3 <= j < 2 * HEADS - 1:
                        turn(j + 1)
                    attend(j)
                wait_dve()
                for m in range(KT):
                    unit_product(ua_hi, ua_lo)
            if do_f2:
                ffn(ub_hi, ub_lo, hidden_a)
            sum_squares(L)
            spread(L)
            assert unit.n == units, (unit.n, units)

        @block.scalar
        def _(act):
            from_dve, to_dve = Tally(s_d2a), Tally(s_a2d)

            def wait_dve():
                act.wait_ge(s_d2a, from_dve.add())

            def run(out, in_, func, last=True, **kw):
                ins = nc.scalar.activation(out, in_, func, **kw)
                if last:
                    to_dve.add()
                    ins.then_inc(s_a2d, 1)
                return ins

            def one(out, in_, func, **kw):
                wait_dve()
                run(out, in_, func, **kw)

            def load(dst, src, s):
                act.dma_start(dst, src).then_inc(s, 16)

            def finished_product(*name):
                act.wait_ge(s_prod, finished[name])
                return ps[(finished[name] - 1) % 4]

            for dst, n in ((gains, "gains"), (ones, "ones"), (ident, "ident"), (pscale, "pool_scale"), (dskip, "dskip"),
                           (edge, "edge"), (eye, "eye")):
                load(dst[:], a[n], s_const)
            if do_mix:
                for k, n in enumerate(("ar", "ai", "ld")):
                    load(PL[n], a["pl_a"][k], s_pl)
                load(prep[:, 512:1536], a["pl_bc"], s_pl)
                load(kexp, a["kexp"], s_pl)
                load(nidx[:], a["nidx"], s_pl)
            for k in range(KT):
                load(h[:, k], a["x"][k], s_x)

            kv_done = [0]

            def kv_high(n):
                for m in range(kv_done[0], kv_done[0] + n if do_att else 0):
                    pair = finished_product("kv", m)
                    hi, _, src = kv_halves(m, pair[:].rearrange("p c n -> p (c n)"))
                    run(hi, src, ACT.Copy)
                    kv_done[0] += 1

            def root(n=L // P):
                one(norm[:, 1, 0:n], norm[:, 0, 0:n], ACT.Sqrt)

            def trig(r, s, c):
                wait_dve()
                run(s, r, ACT.Sin, last=False)
                run(c, r, ACT.Sin, scale=0.5)

            if do_att:
                root(N_MEM // P)
            if do_mix:
                one(PL["t1"], PL["ld"], ACT.Exp)
                one(PL["mag"], PL["dtar"], ACT.Exp)
                trig(PL["rr"], PL["s"], PL["c"])
                kv_high(2)
                wait_dve()
                run(m8[:], PL["dtar"], ACT.Exp, scale=float(T))
                kv_high(1)
                one(k_mag, k_mag, ACT.Exp)
                kv_high(1)
                trig(k_ang, k_s, k_c)

            def store_half(n):
                if do_att:
                    wait_dve()
                    for d, t in ((d_kv_hi, kv_hi), (d_kv_lo, kv_lo)):
                        load(d[n], t[:, n].bitcast(F32), s_kvstore)

            kv_high(KT - kv_done[0])
            store_half(0)
            kv_high(2)
            if do_mix:
                wait_dve()
            store_half(1)
            if do_mix:
                for dr in range(2):
                    wait_dve()
                    load(d_e[:, dr].rearrange("p r c -> p (r c)"), e_out[dr], s_estore)
                load(d_f, ca[:].rearrange("p q c e x -> p q c (e x)"), s_pstore)

            def store_kernels():
                if do_mix:
                    wait_dve()
                    for k in range(2):
                        load(d_k[:, k::2, :], kp[k * HG:(k + 1) * HG].rearrange("p g d x -> p g (d x)"), s_kstore)

            def split_high(m, dst, gi):
                if dst is not None:
                    one(dst[:, m], h[:, m], ACT.Copy, scale=gains[:, gi, m:m + 1])

            def squares(last, between):
                for m in range(KT):
                    if last or m > 2:
                        wait_dve()
                    run(acc[:] if m == 0 else (rn, sq)[m % 2][:], h[:, m], ACT.Square)
                    if m == 2 and between:
                        between()

            def boundary(dst, gi, between=None):
                for m in range(KT):
                    split_high(m, dst, gi)
                squares(dst is None, between)

            def ffn(next_dst, gi, mem, beside=lambda t: None):
                act_hi, _, f_gate, f_silu, _, f_act = mem
                root()

                def hidden(b, t):
                    one(f_silu[:], f_gate[:], ACT.Silu)
                    one(act_hi[:, b, t], f_act[:], ACT.Copy)
                for t in range(2):
                    hidden(0, t)
                    beside(t)
                with act.Fori(0, FT // 4) as i:
                    from_dve.enter(i, 8)
                    to_dve.enter(i, 8)
                    for b in range(2):
                        for t in range(2):
                            hidden(1 - b, t)
                    from_dve.leave(FT // 4)
                    to_dve.leave(FT // 4)
                boundary(next_dst, gi)

            boundary(u_hi, 0, store_kernels)
            def rotations(dr):
                if do_mix:
                    trig(t_r, t_s, t_c)
                    wait_dve()
                    for k, t in enumerate((t_c, t_s)):
                        load(d_tab[:, k, dr * PAIRS:(dr + 1) * PAIRS].rearrange("p c n -> p (c n)"), t, s_pstore)

            def beside_first(t):
                rotations(t)
                if t == 0:
                    store_m()

            def store_m():
                if do_mix:
                    act.wait_ge(s_kstore, 32)
                    for i in range(T):
                        load(d_m[HG * i:HG * (i + 1)], d_k[:, :, (T - 1 - i) * HG:(T - 1 - i) * HG + P], s_mstore)

            if do_f1:
                ffn(after_f1[0], 1, hidden_b, beside_first)
            if do_mix:
                for m in range(KT):
                    load(d_h[m], h[:, m], s_hspill)
                if not do_f1:
                    beside_first(0)
                    beside_first(1)
                root()
                act.wait_ge(s_hspill, 16 * KT)
                load(pw_raw[:], a["pool_w"], s_pw)
                for t in range(2):
                    wait_dve()
                    load(d_s[:, t * P:(t + 1) * P, :].rearrange("i c n -> c i n"), s_perm[:, t], s_sst)
                    if t == 1:
                        act.wait_ge(s_sst, 32)
                        for i in range(T):
                            load(u_t[HG * i:HG * (i + 1)], d_s[i].rearrange("(g c) n -> c g n", c=HG), s_uld)
                act.wait_ge(s_estore, 32)
                act.wait_ge(s_pstore, 80)
                act.wait_ge(s_mstore, 16 * T)

                def load_step(q):
                    e_m, f_m, m_m, tab = step_sets[q % 2]
                    arrived = s_step[q % 2]
                    load(e_m[:], d_e[:, :, :, q * P:(q + 1) * P], arrived)
                    load(m_m[:], d_m[:, 2 * q:2 * q + 2, :], arrived)
                    for dr in range(2):
                        load(f_m[:, :, dr], d_f[:, :, dr * PAIRS + q, (1 - dr) * HG:(1 - dr) * HG + P], arrived)
                        load(tab[:, :, dr], d_tab[:, :, dr * PAIRS + q, :], arrived)

                load_step(0)

                def gate(m):
                    one(merged[:, KT - 1 - m], merged[:, KT - 1 - m], ACT.Sigmoid)

                gate(0)
                wait_dve()
                load_step(1)
                for q in range(PAIRS):
                    if q + 1 < PAIRS:
                        gate(q + 1)
                    wait_dve()
                    load(d_y[:, 2 * q:2 * q + 2, :], y_t[:, q % 2], s_yst[q % 2])
                    if q + 2 < PAIRS:
                        load_step(q + 2)
                for k in range(2):
                    act.wait_ge(s_yst[k], 16 * PAIRS // 2)
                for g in range(G):
                    load(y_in[HG * (g % 8):HG * (g % 8 + 1), g // 8],
                         d_y[:, g, :].rearrange("(i c) n -> c i n", c=HG), s_yld)
                act.wait_ge(s_yld, 16 * G)
                for t in range(2):
                    run(y_g[:, t].rearrange("p (n i) -> p i n", i=T), y_in[:, t], ACT.Gelu_apprx_tanh, last=(t == 1))
                def high(m):
                    run(ua_hi[:, KT - 1 - m], merged[:, KT - 1 - m], ACT.Copy)

                for m in range(KT):
                    if m % 2 == 0:
                        for m2 in range(2):
                            run(z_b[:, m2], finished_product("glu gate", m + m2)[:].rearrange("p c n -> p (c n)"), ACT.Sigmoid)
                    if m == KT - 1:
                        wait_dve()
                        for k in range(5):
                            high(k)
                    one(z_d[:], z_c[:], ACT.Sigmoid)
                for m in range(5, KT - 1):
                    high(m)
                wait_dve()
                high(KT - 1)
                for m in range(KT):
                    load(h[:, m], d_h[m], s_hload)
                boundary(after_mix[0], 2 if do_att else 4)
            if do_att:
                for m in range(KT):
                    load(d_h[m], h[:, m], s_hspill)
                root()
                act.wait_ge(s_hspill, 16 * KT * (2 if do_mix else 1))
                act.wait_ge(s_kvstore, 64)

                def load_k(hd):
                    for src, dst in ((d_kv_hi, k_hi), (d_kv_lo, k_lo)):
                        load(dst[:, hd % 2].bitcast(F32), src[0].rearrange("p (m t) -> p m t", m=KT)[:, 2 * hd:2 * hd + 2],
                             s_k_in[hd % 2])

                def load_v(hd):
                    for src, dst in ((d_kv_hi, v_hi), (d_kv_lo, v_lo)):
                        load(dst[:, hd % 2].bitcast(F32), src[1].rearrange("p (m d) -> p m d", m=2)[:, :, hd * HD:(hd + 1) * HD],
                             s_v_in[hd % 2])
                for hd in range(2):
                    load_k(hd)
                    load_v(hd)

                def split_q(m):
                    one(ua_hi[:, m], sq[:], ACT.Copy)

                def softmax(j):
                    wait_dve()
                    pair = finished_product("scores", j)
                    for t in range(4):
                        run(prob[:, j % 2, t], pair[:, t // 2, (t % 2) * N_MEM:(t % 2 + 1) * N_MEM], ACT.Exp,
                            last=(t == 3), bias=stat[:, j % 2, 1, t:t + 1], scale=HD ** -0.5, accum_out=stat[:, j % 2, 2, t:t + 1])
                    if j % 2 == 1 and j // 2 + 2 < HEADS:
                        load_k(j // 2 + 2)

                def turned(j):
                    run(pt(j)[0], finished_product("turn", j)[:], ACT.Copy)

                for m in range(4):
                    split_q(m)
                softmax(0)
                split_q(4)
                softmax(1)
                for j in range(2 * HEADS):
                    if j + 2 < 2 * HEADS:
                        turned(j)
                        softmax(j + 2)
                    if j < 3:
                        split_q(5 + j)
                    if 2 * HEADS - 3 <= j < 2 * HEADS - 1:
                        turned(j + 1)
                    hd, cols = j // 2, slice(j % 2 * HALF, (j % 2 + 1) * HALF)
                    run(ua_hi[:, 2 * hd:2 * hd + 2, cols], finished_product("attend", j)[:], ACT.Copy)
                    if j % 2 == 1 and j // 2 + 2 < HEADS:
                        load_v(j // 2 + 2)
                wait_dve()
                for m in range(KT):
                    load(h[:, m], d_h[m], s_hload)
                boundary(after_att[0], 4)
            if do_f2:
                ffn(None, 0, hidden_a)
            root()
            for m in range(KT):
                wait_dve()
                load(a["out"][m], h[:, m], s_out)
            act.wait_ge(s_out, 16 * KT)

        @block.vector
        def _(dve):
            step, prod, free = Tally(s_dve), Tally(s_prod), Tally(s_free)
            to_act, from_act, to_pe = Tally(s_d2a), Tally(s_a2d), Tally(s_d2p)
            norms = Tally(s_norm)
            all_tallies = (step, prod, free, to_act, from_act, to_pe)
            v = nc.vector

            def link(ins, tally=step):
                tally.add()
                ins.then_inc(tally.sem, 1)
                dve.wait_ge(tally.sem, tally.at())

            def wait_act():
                dve.wait_ge(s_a2d, from_act.add())

            def pair_of():
                return ps[(prod.n - 1) % 4]

            held = []

            def wait_product():
                if held:
                    if held[0] is not None:
                        return held.pop(0)
                    held.pop(0)
                    first(free)
                dve.wait_ge(s_prod, prod.add())
                return pair_of()[:].rearrange("p c n -> p (c n)")

            def tt(out, x, y, op=ALU.mult, tally=step):
                link(v.tensor_tensor(out, x, y, op), tally)

            def ts(out, x, s1, s2=None, op0=ALU.mult, op1=None, tally=step):
                if op1 is None:
                    link(v.tensor_scalar(out, x, s1, None, op0), tally)
                else:
                    link(v.tensor_scalar(out, x, s1, s2, op0, op1), tally)

            def stt(out, x, s, y, op0, op1, tally=step):
                link(v.scalar_tensor_tensor(out=out, in0=x, scalar=s, in1=y, op0=op0, op1=op1), tally)

            def cp(out, x, tally=step):
                link(v.tensor_copy(out, x), tally)

            def rounded(r, ang, k):
                ts(k, ang, INV_2PI, ROUND, ALU.mult, ALU.add)
                ts(k, k, ROUND, None, ALU.subtract)
                stt(r, k, -TWO_PI_HI, ang, ALU.mult, ALU.add)
                stt(r, k, -TWO_PI_LO, r, ALU.mult, ALU.add)
                ts(r, r, PI_IN, -PI_IN, ALU.min, ALU.max, tally=to_act)

            def cosine(c):
                wait_act()
                tt(c, c, c)
                ts(c, c, -2.0, 1.0, ALU.mult, ALU.add)

            def root_factor(w, keep=True):
                n = w // P
                dve.wait_ge(s_norm, norms.add())
                pair = ps[(prod.n % 4)]
                x, root, y, z = (norm[:, k, 0:n] for k in range(4))
                ts(x, pair[:, 0, 0:n], 1.0 / D, EPS, ALU.mult, ALU.add, tally=to_act)
                wait_act()
                link(v.reciprocal(y, root))
                tt(z, y, y)
                tt(z, z, x)
                ts(z, z, -0.5, 1.5, ALU.mult, ALU.add)
                tt(y, y, z)
                cp(norm_hi[:, 0:n], y)
                tt(z, y, norm_hi[:, 0:n].bitcast(F32), ALU.subtract)
                for out, half, tally in ((diag_hi, norm_hi[:, 0:n].bitcast(F32), step), (diag_lo, z, to_pe)):
                    tt(out[:, 0:w].rearrange("p (c t) -> p c t", c=n), ident[:].unsqueeze(1).to_broadcast([P, n, P]),
                       half.unsqueeze(2).to_broadcast([P, n, P]), tally=tally)
                pair = wait_product()[:, 0:w]
                if keep:
                    cp(rn[:, 0:w], pair)
                return pair

            def discretise(q):
                wait_act()
                tt(q["dtar"], q["t1"], q["ar"], tally=to_act)
                tt(q["t2"], q["t1"], q["ai"])
                wait_act()
                rounded(q["rr"], q["t2"], q["t3"])
                tt(q["t1"], q["ar"], q["ar"])
                tt(q["t2"], q["ai"], q["ai"])
                tt(q["t1"], q["t1"], q["t2"], ALU.add)
                link(v.reciprocal(q["t4"], q["t1"]))
                cosine(q["c"])
                tt(q["t1"], q["mag"], q["c"])
                ts(q["t1"], q["t1"], 1.0, None, ALU.subtract)
                tt(q["t2"], q["mag"], q["s"])
                tt(q["qr"], q["t1"], q["ar"])
                tt(q["t3"], q["t2"], q["ai"])
                tt(q["qr"], q["qr"], q["t3"], ALU.add)
                tt(q["qr"], q["qr"], q["t4"])
                tt(q["qi"], q["t2"], q["ar"])
                tt(q["t3"], q["t1"], q["ai"])
                tt(q["qi"], q["qi"], q["t3"], ALU.subtract)
                tt(q["qi"], q["qi"], q["t4"])

            def complex_mult(re, im, ar, ai, br, bi, tmp, neg_im=False, tally=step, beside=lambda: None):
                tt(re, ar, br)
                tt(tmp, ai, bi)
                tt(re, re, tmp, ALU.subtract)
                beside()
                tt(im, ar, bi)
                tt(tmp, ai, br)
                if neg_im:
                    stt(im, im, -1.0, tmp, ALU.mult, ALU.subtract, tally=tally)
                else:
                    tt(im, im, tmp, ALU.add, tally=tally)

            def first(tally=to_act):
                link(v.memset(stat[:, 0, 3, 0:1], 0.0), tally)

            if do_att:
                dve.wait_ge(s_mem, 16)
                tt(mem_w[:], mem_t[:], mem_t[:])
            dve.wait_ge(s_const, 16 * 7)
            cp(ones_r[:], ones[:])
            if do_att:
                link(v.tensor_reduce(acc[:, 0:N_MEM], mem_w[:].rearrange("p k t -> p t k"), AX, ALU.add), to_pe)
                root_factor(N_MEM)
                first(free)
                for k in range(KT):
                    stt(mem_w[:, k], mem_t[:, k], gains[:, 3, k:k + 1], rn[:, 0:N_MEM], ALU.mult, ALU.mult)
                    cp(mn_hi[:, k], mem_w[:, k])
                    tt(mn_lo[:, k], mem_w[:, k], mn_hi[:, k].bitcast(F32), ALU.subtract, tally=to_pe)
            kv_left = list(range(KT + 2)) if do_att else []

            def store_kv():
                if not kv_left:
                    return
                m = kv_left.pop(0)
                pair = wait_product()
                hi, lo, src = kv_halves(m, pair)
                wait_act()
                tt(lo, src, hi.bitcast(F32), ALU.subtract, tally=free)
                if m in (KT - 1, KT + 1):
                    first()

            if do_mix:
                q = PL
                dve.wait_ge(s_pl, 96)
                first()
                discretise(q)
                store_kv()
                store_kv()
                bro = lambda t: t.unsqueeze(2).to_broadcast([P, COLS, HG])
                complex_mult(p_bb[:, 0], p_bb[:, 1], bro(q["qr"]), bro(q["qi"]), p_b[:, 0], p_b[:, 1],
                             prep[:, tmp_at:tmp_at + COLS * HG].rearrange("p (c x) -> p c x", c=COLS))
                for x in range(2):
                    link(v.memset(p_bd[x].rearrange("p c g x -> p (c g x)"), 0.0))
                    for g in range(2):
                        rows = slice(g * S, (g + 1) * S)
                        cp(p_bd[x][rows, :, g], p_bb[rows, x])
                ts(q["t4"], q["rr"], float(T), None)
                ts(q["t3"], q["t4"], INV_2PI, ROUND, ALU.mult, ALU.add)
                ts(q["t3"], q["t3"], ROUND, None, ALU.subtract)
                stt(turn8[:], q["t3"], -TWO_PI_HI, q["t4"], ALU.mult, ALU.add)
                stt(turn8[:], q["t3"], -TWO_PI_LO, turn8[:], ALU.mult, ALU.add, tally=to_act)
                wait_act()
                store_kv()
                e3 = lambda t: t.rearrange("p (c e) -> p c e", c=COLS)
                be = lambda t: t.unsqueeze(2).to_broadcast([P, COLS, T + 1])
                tt(e3(k_mag), e3(kexp), be(q["dtar"]), tally=to_act)
                tt(e3(k_t), e3(kexp), be(q["rr"]))
                wait_act()
                rounded(k_ang, k_t, k_c)
                store_kv()
                cosine(k_c)
                tt(k_s, k_s, k_mag)
                tt(k_c, k_c, k_mag)
                store_kv()
                for dr in range(2):
                    cols = slice(dr * PAIRS, (dr + 1) * PAIRS)
                    shape = [P, PAIRS, T, HG]
                    pw = [(e3(k)[:, cols, T - 1::-1] if dr == 0 else e3(k)[:, cols, T:0:-1]).unsqueeze(3).to_broadcast(shape)
                          for k in (k_c, k_s)]
                    bb = [p_bb[:, x, cols].unsqueeze(2).to_broadcast(shape) for x in range(2)]
                    work = prep[:, tmp_at:tmp_at + PAIRS * P].rearrange("p (c e x) -> p c e x", c=PAIRS, e=T)
                    complex_mult(ee[:, 0, cols], ee[:, 1, cols], *pw, *bb, work, tally=to_pe if dr else step,
                                 beside=store_kv)
                    if dr == 0:
                        store_kv()
                w4 = lambda t: e3(t).unsqueeze(3).to_broadcast([P, COLS, T + 1, HG])
                c4 = lambda k: p_b[:, k].unsqueeze(2).to_broadcast([P, COLS, T + 1, HG])
                complex_mult(ca[:, 0], ca[:, 1], w4(k_c), w4(k_s), c4(2), c4(3), ca_t, neg_im=True, tally=to_act)
                first(to_pe)
            while kv_left:
                store_kv()
            if do_mix:
                for dr in range(2):
                    for ri in range(2):
                        pair = wait_product()
                        cp(e_out[dr][:, ri * D:(ri + 1) * D], pair, tally=free)
                    first()

            def kernels_out(dr):
                wait_product()
                src = pair_of()[0:2 * HG].rearrange("p c (g e x) -> p (c g) e x", g=4, e=T)
                if dr == 0:
                    cp(kp[:, :, T - 1:DIAGS], src, tally=free)
                else:
                    cp(kp[:, :, 0:T - 1], src[:, :, 0:T - 1])
                    tt(kp[:, :, T - 1], kp[:, :, T - 1], src[:, :, T - 1], ALU.add, tally=free)

            def skip_connection():
                for p in range(PAIRS):
                    stt(kp[:, p, T - 1], eye[:], dskip[:, p:p + 1], kp[:, p, T - 1], ALU.mult, ALU.add,
                        tally=to_act if p == PAIRS - 1 else step)

            def boundary(dst_hi, dst_lo, gi, new=None, between=None):
                def low(m):
                    wait_act()
                    stt(dst_lo[:, m], h[:, m], gains[:, gi, m:m + 1], dst_hi[:, m].bitcast(F32),
                        ALU.mult, ALU.subtract, tally=to_pe)

                def add(m):
                    wait_act()
                    if m:
                        tt(acc[:], acc[:], (rn, sq)[m % 2][:], ALU.add,
                           tally=to_pe if m == KT - 1 else to_act if dst_hi is not None and m + 2 < KT else step)

                for m in range(KT):
                    if new:
                        new(m)
                    first()
                    if m:
                        (low if dst_hi is not None else add)(m - 1)
                if dst_hi is None:
                    add(KT - 1)
                else:
                    low(KT - 1)
                    if between:
                        between()
                    for m in range(KT):
                        add(m)

            def beside_x(m):
                if m == 1 and do_att:
                    dve.wait_ge(s_kvstore, 64)
                if m == 4 and do_mix:
                    kernels_out(0)

            def last_kernels():
                kernels_out(1)
                skip_connection()

            dve.wait_ge(s_x, 16 * KT)
            boundary(u_hi, u_lo, 0, beside_x, last_kernels if do_mix else None)

            def rotations(dr):
                if do_mix:
                    dve.wait_ge(s_pstore, 16 if dr == 0 else 48)
                    dve.wait_ge(s_estore, 32)
                    cols = slice(dr * PAIRS, (dr + 1) * PAIRS)
                    tt(t_c.rearrange("p (c n) -> p c n", c=PAIRS), turn8[:, cols].unsqueeze(2).to_broadcast([P, PAIRS, NC]),
                       nidx[:].unsqueeze(1).to_broadcast([P, PAIRS, NC]))
                    rounded(t_r, t_c, t_s)
                    cosine(t_c)
                    first()

            def residual(m, coef):
                pair = wait_product()
                link(v.scalar_tensor_tensor(out=h[:, m], in0=pair, scalar=coef, in1=h[:, m], op0=ALU.mult, op1=ALU.add), free)

            def opening(spare, evacuate):
                if do_mix:
                    dve.wait_ge(s_pstore, 16)
                    dve.wait_ge(s_estore, 32)
                    dve.wait_ge(s_kstore, 32)
                cp(spare, wait_product(), tally=free)
                prod.add(2)
                pairs = [ps[(prod.n - 2 + k) % 4][:].rearrange("p c n -> p (c n)") for k in range(2)]
                root_factor(L)
                evacuate(spare, rn[:], step)
                held.extend(pairs + [None])

            def ffn(next_hi, next_lo, gi, mem, beside=lambda t: None):
                act_hi, act_lo, f_gate, f_silu, f_up, f_act = mem

                def gate(pair, factor, tally):
                    tt(f_gate[:], pair, factor, tally=tally)
                    first()

                def hidden(b, t, first_product=False):
                    if not first_product:
                        gate(wait_product(), rn[:], free)
                    pair = wait_product()
                    tt(f_up[:], pair, rn[:], tally=free)
                    wait_act()
                    tt(f_act[:], f_silu[:], f_up[:], tally=to_act)
                    wait_act()
                    tt(act_lo[:, b, t], f_act[:], act_hi[:, b, t].bitcast(F32), ALU.subtract, tally=to_pe)

                opening(f_gate[:], gate)
                for t in range(2):
                    hidden(0, t, t == 0)
                    beside(t)
                with dve.Fori(0, FT // 4) as i:
                    for t, stride in zip(all_tallies, (0, 24, 24, 8, 8, 4)):
                        t.enter(i, stride)
                    for b in range(2):
                        for t in range(2):
                            hidden(1 - b, t)
                        for m in range(KT):
                            residual(m, 0.5)
                    for t in all_tallies:
                        t.leave(FT // 4)
                boundary(next_hi, next_lo, gi, lambda m: residual(m, 0.5))

            if do_f1:
                ffn(*after_f1, 1, hidden_b, rotations)
            if do_mix:
                def s_out(t, pair, factor, tally):
                    tt(s_perm[:, t].rearrange("p i n -> p n i"), pair.rearrange("p (n i) -> p n i", i=T),
                       factor.rearrange("p (n i) -> p n i", i=T), tally=tally)
                    first()

                if not do_f1:
                    rotations(0)
                    rotations(1)
                def first_s(pair, factor, tally):
                    dve.wait_ge(s_hspill, 16 * KT)
                    s_out(0, pair, factor, tally)

                opening(mx_a[:, 0:L], first_s)
                s_out(1, wait_product(), rn[:], free)
                dve.wait_ge(s_pstore, 80)
                dve.wait_ge(s_pw, 16)
                cp(pw_hi[:], pw_raw[:])
                tt(pw_lo[:], pw_raw[:], pw_hi[:].bitcast(F32), ALU.subtract)
                for t in (mx_v, mx_a, mx_b):
                    link(v.memset(t[:, 0:PAD], 0.0))
                    link(v.memset(t[:, PAD + L:], 0.0))

                def pool(g):
                    pair = wait_product()
                    w = WINDOWS[g]
                    tt(mx_v[:, PAD:PAD + L], pair, rn[:], tally=free)
                    n = L + 2 * PAD
                    tt(mx_a[:, 1:n], mx_v[:, 0:n - 1], mx_v[:, 1:n], ALU.add)
                    cur, nxt, size = mx_a, mx_b, 2
                    while size < w:
                        k = size // 2
                        tt(nxt[:, k:n - k], cur[:, 0:n - 2 * k], cur[:, 2 * k:n], ALU.add)
                        cur, nxt, size = nxt, cur, 2 * size
                    for side in range(2):
                        cols = slice(PAD, 2 * PAD) if side == 0 else slice(L, L + PAD)
                        tt(cur[:, cols], cur[:, cols], edge[:, g, side])
                    stt(nxt[:, PAD:PAD + L], cur[:, PAD:PAD + L], 1.0 / w, mx_v[:, PAD:PAD + L], ALU.mult, ALU.subtract)
                    hi, lo = pooled[:, g % 2, 0], pooled[:, g % 2, 1]
                    cp(hi, nxt[:, PAD:PAD + L])
                    tt(lo, nxt[:, PAD:PAD + L], hi.bitcast(F32), ALU.subtract, tally=to_pe)

                scaled = acc

                def pool_mixed(g):
                    pair = wait_product()
                    ts(scaled[:], pair, pscale[:, g:g + 1], tally=free)
                    cp(mixed_hi[:, g], scaled[:])
                    tt(mixed_lo[:, g], scaled[:], mixed_hi[:, g].bitcast(F32), ALU.subtract)
                pool(0)
                pool(1)
                pool_mixed(0)
                pool(2)
                pool_mixed(1)
                pool(3)

                def gate(m):
                    tt(merged[:, KT - 1 - m], wait_product(), rn[:], tally=free)
                    first()

                def project(m):
                    tt(merged[:, KT - 1 - m], merged[:, KT - 1 - m], wait_product(), tally=free)

                gate(0)
                link(v.memset(sx[:], 0.0))
                dve.wait_ge(s_uld, 16 * T)
                for q in range(PAIRS):
                    dve.wait_ge(s_step[q % 2], 96 * (q // 2 + 1))
                    tab = step_sets[q % 2][3]
                    first(to_pe)
                    if q == 0:
                        pool_mixed(2)
                        pool_mixed(3)
                        first()
                        wait_act()
                    pair = wait_product()
                    re, im = (pair[:, k * HALF:k * HALF + 2 * NC].rearrange("p (d n) -> p d n", d=2) for k in range(2))
                    ct, sn = tab[:, 0], tab[:, 1]
                    tt(sw[:, 0], re, ct)
                    tt(st_[:, 0], im, sn)
                    tt(sw[:, 0], sw[:, 0], st_[:, 0], ALU.add)
                    tt(sw[:, 1], im, ct)
                    tt(st_[:, 0], re, sn, tally=free)
                    tt(sw[:, 1], sw[:, 1], st_[:, 0], ALU.subtract)
                    for dr in range(2):
                        mag = m8[:, dr * PAIRS + q:dr * PAIRS + q + 1].to_broadcast([P, NC])
                        for ri in range(2):
                            link(v.tensor_tensor_scan(st_[:, ri, dr], mag, sw[:, ri, dr], 0.0, ALU.mult, ALU.add))
                    tt(sw[:, 0], st_[:, 0], ct)
                    tt(sw[:, 1], st_[:, 1], sn)
                    tt(sx[:, 0, :, 1:], sw[:, 0], sw[:, 1], ALU.subtract)
                    tt(sw[:, 0], st_[:, 1], ct)
                    tt(sw[:, 1], st_[:, 0], sn)
                    tt(sx[:, 1, :, 1:], sw[:, 0], sw[:, 1], ALU.add, tally=to_pe)
                    if q + 1 < PAIRS:
                        gate(q + 1)
                    else:
                        project(0)
                        project(1)
                    pair = wait_product()
                    if q >= 2:
                        dve.wait_ge(s_yst[q % 2], 16 * (q // 2))
                    cp(y_t[:, q % 2], pair.rearrange("p (g n) -> p g n", g=2)[:, :, 0:NC], tally=free)
                    first()
                    if q + 1 < PAIRS:
                        wait_act()
                for m in range(2, KT):
                    if m == KT - 2:
                        wait_act()
                        cp(y_hi[:], y_g[:])
                        tt(y_lo[:], y_g[:], y_hi[:].bitcast(F32), ALU.subtract, tally=to_pe)
                    project(m)

                def merged_low(m):
                    wait_act()
                    at = KT - 1 - m
                    tt(ua_lo[:, at], merged[:, at], ua_hi[:, at].bitcast(F32), ALU.subtract, tally=to_pe)

                for m in range(KT):
                    if m % 2 == 0:
                        for m2 in range(2):
                            wait_product()
                            wait_act()
                            first(free)
                            tt(z_a[:, m2], wait_product(), z_b[:, m2], tally=free)
                    pair = wait_product()
                    if m == KT - 1:
                        first()
                    tt(z_c[:], pair, rn[:], tally=free)
                    first()
                    if m == KT - 1:
                        for k in range(5):
                            merged_low(k)
                    wait_act()
                    tt(z_d[:], z_d[:], z_a[:, m % 2])
                    tt(merged[:, KT - 1 - m], merged[:, KT - 1 - m], z_d[:], ALU.add)
                first()
                for m in range(5, KT):
                    merged_low(m)
                dve.wait_ge(s_hload, 16 * KT)
                boundary(*after_mix, 2 if do_att else 4, lambda m: residual(m, 1.0))
            if do_att:
                q_ready = Tally(s_q)

                def evac_q(m, product=None, factor=rn[:], tally=free):
                    tt(sq[:], wait_product() if product is None else product, factor, tally=tally)
                    first()
                    wait_act()
                    tt(ua_lo[:, m], sq[:], ua_hi[:, m].bitcast(F32), ALU.subtract, tally=q_ready)

                probs = Tally(s_prob)

                def scores_max(j):
                    pair = wait_product()
                    assert prod.n == finished["scores", j]
                    low = stat[:, j % 2]
                    link(v.tensor_reduce(low[:, 0], pair.rearrange("p (t n) -> p t n", t=4), AX, ALU.max))
                    ts(low[:, 1], low[:, 0], -(HD ** -0.5), None, tally=to_act)

                def scores_read():
                    wait_act()
                    first(free)

                def normalise(j):
                    low = stat[:, j % 2]
                    link(v.reciprocal(low[:, 0], low[:, 2]))
                    tt(prob[:, j % 2], prob[:, j % 2], low[:, 0].unsqueeze(2).to_broadcast([P, 4, N_MEM]), tally=probs)

                def low_half(lo, hi):
                    pair = wait_product()
                    wait_act()
                    tt(lo, pair.rearrange("p (c n) -> p c n", c=2), hi.bitcast(F32), ALU.subtract, tally=free)

                opening(hidden_a[2][:], lambda *args: evac_q(0, *args))
                for m in range(1, 4):
                    evac_q(m)
                scores_max(0)
                scores_read()
                normalise(0)
                evac_q(4)
                scores_max(1)
                scores_read()
                def turned(j):
                    low_half(*reversed(pt(j)))
                    first(to_pe)

                for j in range(2 * HEADS):
                    if j + 2 < 2 * HEADS:
                        turned(j)
                        scores_max(j + 2)
                        normalise(j + 1)
                        scores_read()
                    if j < 3:
                        evac_q(5 + j)
                    if j == 2 * HEADS - 3:
                        normalise(j + 2)
                    if 2 * HEADS - 3 <= j < 2 * HEADS - 1:
                        turned(j + 1)
                    hd, cols = j // 2, slice(j % 2 * HALF, (j % 2 + 1) * HALF)
                    low_half(ua_lo[:, 2 * hd:2 * hd + 2, cols], ua_hi[:, 2 * hd:2 * hd + 2, cols])
                first()
                first(to_pe)
                dve.wait_ge(s_hload, 16 * KT * (2 if do_mix else 1))
                boundary(*after_att, 4, lambda m: residual(m, 1.0))
            if do_f2:
                ffn(None, None, 0, hidden_a)
            factor = root_factor(L, keep=False)
            for m in range(KT):
                stt(h[:, m], h[:, m], gains[:, 5, m:m + 1], factor, ALU.mult, ALU.mult, tally=to_act)


def stages_units(stages):
    out = []
    if "A" in stages:
        out += [("k", m) for m in range(KT)] + [("v", k) for k in range(KT)]
    def ffn(f):
        gu = lambda j: [(f"{f}_w_gate", j), (f"{f}_w_up", j)]
        seq = gu(0) + gu(1)
        for i in range(1, FT // 2):
            seq += gu(2 * i) + gu(2 * i + 1) + [(f"{f}_down", 2 * i - 2), (f"{f}_down", 2 * i - 1)]
        return seq + [(f"{f}_down", FT - 2), (f"{f}_down", FT - 1)]
    if "1" in stages:
        out += ffn("ffn1")
    if "M" in stages:
        out += [("w_in", 4), ("w_in", 5)] + [("w_in", m) for m in range(4)]
        out += [("w_in", 6 + m) for m in range(KT)]
        out += [("pool_proj", j) for j in range(KT // 2)]
        for j in range(KT // 2):
            out += [("glu", j), ("w_in", 14 + 2 * j), ("w_in", 15 + 2 * j)]
        out += [("mix_out", m) for m in range(KT)]
    if "A" in stages:
        out += [("w_q", m) for m in range(KT)] + [("w_xo", m) for m in range(KT)]
    if "2" in stages:
        out += ffn("ffn2")
    return out


def pack(inputs, stages):
    w = {k: np.asarray(x)[0] for k, x in inputs.items() if k.startswith(("w_", "ffn")) and np.asarray(x).ndim == 3}

    def cols(x, m, width=P):
        kt = x.shape[0] // P
        return x[:, m * P:(m + 1) * P].reshape(kt, P, P).transpose(1, 0, 2).reshape(P, kt * P)

    out = np.empty((len(stages_units(stages)), P, D), np.float32)
    for u, (n, m) in enumerate(stages_units(stages)):
        if n == "k":
            t = cols(w["w_kv"], m)
        elif n == "v":
            t = w["w_kv"][m * P:(m + 1) * P, D:]
        elif n.endswith("_down"):
            t = w[n[:4] + "_w_down"][m * P:(m + 1) * P]
        elif n == "pool_proj":
            t = np.concatenate([cols(w["w_pool_proj"], 2 * m + q) for q in range(2)], 1)
        elif n == "glu":
            t = np.concatenate([cols(w[x], 2 * m + q) for q in range(2) for x in ("w_glu_gate", "w_glu_val")], 1)
        elif n == "mix_out":
            t = cols(w["w_mix_out"], m).reshape(P, KT, P)[:, ::-1].reshape(P, D)
        else:
            t = cols(w[n], m)
        out[u] = t
    return out


STAGES = "1MA2"


def kernel(**inputs):
    from concourse import bacc
    from concourse.bass_utils import run_bass_kernel_spmd

    f = {k: np.asarray(x) for k, x in inputs.items()}
    A = np.ascontiguousarray
    arrays = {"weights": pack(inputs, STAGES)}
    arrays["x"] = A(f["x"][0].T.reshape(KT, P, L))
    arrays["mem"] = A(f["mem"][0].T.reshape(KT, P, N_MEM).transpose(1, 0, 2))
    norms = [f["ffn1_norm"][0], f["mix_norm"][0], f["xattn_norm"][0], f["mem_norm"][0], f["ffn2_norm"][0], f["final_norm"]]
    arrays["gains"] = A(np.stack(norms).reshape(6, KT, P).transpose(2, 0, 1))
    arrays["pool_scale"] = A(f["pool_scale"][0].reshape(4, P).T)
    arrays["pool_w"] = A(f["pool_w"][0].transpose(1, 0, 2))
    arrays["dskip"] = A(f["ssm_d"][0].reshape(PAIRS, 2 * HG).T)
    ar, ai = f["ssm_a_re"][0], f["ssm_a_im"][0]
    ld = np.broadcast_to(f["ssm_log_dt"][0][:, :, None], ar.shape)
    pl = lambda x: x.reshape(2, PAIRS, P).transpose(2, 0, 1).reshape(P, COLS)
    arrays["pl_a"] = A(np.stack([pl(x) for x in (ar, ai, ld)]))
    bp = [f[k][0].reshape(2, PAIRS, P, HG) for k in ("ssm_b_re", "ssm_b_im")]
    cp = [f[k][0].transpose(0, 1, 3, 2).reshape(2, PAIRS, P, HG) for k in ("ssm_c_re", "ssm_c_im")]
    arrays["pl_bc"] = A(np.stack([x.transpose(2, 0, 1, 3).reshape(P, COLS * HG) for x in bp + cp], 1).reshape(P, -1))
    e = np.arange(T + 1, dtype=np.float32)
    ke = np.stack([e, T - e])[:, None, :]
    arrays["kexp"] = A(np.broadcast_to(np.broadcast_to(ke, (2, PAIRS, T + 1)).reshape(1, -1), (P, COLS * (T + 1))))
    arrays["nidx"] = A(np.broadcast_to(np.arange(NC, dtype=np.float32), (P, NC)))
    arrays["ones"], arrays["ident"] = np.ones((P, P), np.float32), np.eye(P, dtype=np.float32)
    arrays["eye"] = np.tile(np.eye(HG, dtype=np.float32), (2, 1))
    edge = np.empty((4, 2, PAD), np.float32)
    for g, w in enumerate(WINDOWS):
        for side, t in enumerate((np.arange(PAD), np.arange(L - PAD, L))):
            count = np.minimum(t + w - w // 2, L) - np.maximum(t - w // 2, 0)
            edge[g, side] = w / count
    arrays["edge"] = A(np.broadcast_to(edge, (P, 4, 2, PAD)))

    nc = bacc.Bacc("TRN2", target_bir_lowering=False, num_devices=1)
    aps = {n: nc.dram_tensor(f"in_{n}", x.shape, F32, kind="ExternalInput").ap() for n, x in arrays.items()}
    aps["out"] = nc.dram_tensor("out", (KT, P, L), F32, kind="ExternalOutput").ap()
    build(nc, aps, STAGES)
    r = run_bass_kernel_spmd(nc, [{f"in_{n}": x for n, x in arrays.items()}], core_ids=[0])
    return r.results[0]["out"].reshape(D, L).T.reshape(1, L, D)
```
